# Optimizing a Trainium2 kernel written in Bass

```python
import math
import jax, jax.numpy as jnp
from jax import lax
import numpy as np

D_MODEL = 1024
BATCH = 1
SEQ = 512
DEPTH = 1
DEC_BATCH = 8
DEC_SEQ = 1
PAST_LEN = 4096
PAGE_SIZE = 128

MLA_HEADS = 8
MLA_NOPE = 64
MLA_ROPE = 32
MLA_V = 64
KV_RANK = 128
ROPE_THETA = 10000.0
FOX_HEADS = 8
FOX_DIM = 64
D_MIX = MLA_HEADS * MLA_V + FOX_HEADS * FOX_DIM
Q_BLOCK = 128
SPLITS = (MLA_HEADS * MLA_NOPE, MLA_HEADS * MLA_ROPE, KV_RANK, MLA_ROPE,
          FOX_HEADS * FOX_DIM, FOX_HEADS * FOX_DIM, FOX_HEADS * FOX_DIM, FOX_HEADS)
D_IN_PROJ = MLA_HEADS * (MLA_NOPE + MLA_ROPE) + KV_RANK + MLA_ROPE + 3 * FOX_HEADS * FOX_DIM + FOX_HEADS
PEER_HEADS = 8
PEER_KEYS = 128
PEER_EXPERTS = PEER_KEYS * PEER_KEYS
PEER_DKEY = 256
PEER_TOPK = 16
PEER_BLOCK = 128
NORM_EPS = 1e-6
NEG_INF = -1e30

kernel_name = 'hybrid_mla_fox_peer_step'

def rmsnorm(x, g):
    x32 = x.astype(jnp.float32)
    y = x32 * lax.rsqrt(jnp.mean(x32 * x32, axis=-1, keepdims=True) + NORM_EPS)
    return (y * g.astype(jnp.float32)).astype(x.dtype)

def rope(x, pos):
    half = MLA_ROPE // 2
    inv = jnp.power(ROPE_THETA, -jnp.arange(half, dtype=jnp.float32) / half)
    ang = pos.astype(jnp.float32)[:, None] * inv
    if x.ndim == 4:
        ang = ang[:, None, :]
    cos, sin = jnp.cos(ang), jnp.sin(ang)
    x32 = x.astype(jnp.float32)
    x1, x2 = x32[..., :half], x32[..., half:]
    return jnp.concatenate([x1 * cos - x2 * sin, x1 * sin + x2 * cos], axis=-1).astype(x.dtype)

def causal_block_attention(q_parts, k_parts, v, q_pos, k_pos, scale, c_q=None, c_k=None):
    B, T, H, _ = q_parts[0].shape
    qb = min(Q_BLOCK, T)
    nb = T // qb

    def blocks(a):
        return jnp.swapaxes(a.reshape((B, nb, qb) + a.shape[2:]), 0, 1)

    xs = (tuple(blocks(q) for q in q_parts), q_pos.reshape(nb, qb))
    if c_q is not None:
        xs = xs + (blocks(c_q),)
        ck = jnp.transpose(c_k, (0, 2, 1))[:, :, None, :]

    def one_block(args):
        qs, pos = args[0], args[1]
        s = None
        for qi, ki in zip(qs, k_parts):
            spec = 'bqhd,bsd->bhqs' if ki.ndim == 3 else 'bqhd,bshd->bhqs'
            term = jnp.einsum(spec, qi, ki, preferred_element_type=jnp.float32)
            s = term if s is None else s + term
        s = s * scale
        if c_q is not None:
            s = s + jnp.transpose(args[2].astype(jnp.float32), (0, 2, 1))[..., None] - ck
        mask = k_pos[None, :] <= pos[:, None]
        s = jnp.where(mask[None, None], s, NEG_INF)
        p = jax.nn.softmax(s, axis=-1)
        return jnp.einsum('bhqs,bshd->bqhd', p.astype(v.dtype), v)

    out = lax.map(one_block, xs)
    return jnp.swapaxes(out, 0, 1).reshape(B, T, H, v.shape[-1])

def token_mixers(xn, past, w_in, b_forget, g_q_nope, g_q_pe, g_ckv, g_k_pe, w_ukv, g_k_nope,
                 g_fox_q, g_fox_k, g_out_mla, g_out_fox, w_o):
    B, T, _ = xn.shape
    n_past = 0 if past is None else past[0].shape[1]
    pos = n_past + jnp.arange(T, dtype=jnp.int32)
    proj = jnp.einsum('btd,de->bte', xn, w_in)
    split_points = np.cumsum(SPLITS)[:-1].tolist()
    q_nope, q_pe, ckv, kpe, fq, fk, fv, f_logit = jnp.split(proj, split_points, axis=-1)
    q_nope = rmsnorm(q_nope.reshape(B, T, MLA_HEADS, MLA_NOPE), g_q_nope)
    q_pe = rope(rmsnorm(q_pe.reshape(B, T, MLA_HEADS, MLA_ROPE), g_q_pe), pos)
    ckv = rmsnorm(ckv, g_ckv)
    kpe = rope(rmsnorm(kpe, g_k_pe), pos)
    fq = rmsnorm(fq.reshape(B, T, FOX_HEADS, FOX_DIM), g_fox_q)
    fk = rmsnorm(fk.reshape(B, T, FOX_HEADS, FOX_DIM), g_fox_k)
    fv = fv.reshape(B, T, FOX_HEADS, FOX_DIM)
    logf = jax.nn.log_sigmoid((f_logit + b_forget).astype(jnp.float32))
    if past is None:
        ckv_all, kpe_all, fk_all, fv_all, logf_all = ckv, kpe, fk, fv, logf
    else:
        p_ckv, p_kpe, p_fk, p_fv, p_logf = past
        ckv_all = jnp.concatenate([p_ckv, ckv], axis=1)
        kpe_all = jnp.concatenate([p_kpe, kpe], axis=1)
        fk_all = jnp.concatenate([p_fk, fk], axis=1)
        fv_all = jnp.concatenate([p_fv, fv], axis=1)
        logf_all = jnp.concatenate([p_logf.astype(jnp.float32), logf], axis=1)
    S = n_past + T
    k_pos = jnp.arange(S, dtype=jnp.int32)
    kv = jnp.einsum('bsr,re->bse', ckv_all, w_ukv).reshape(B, S, MLA_HEADS, MLA_NOPE + MLA_V)
    k_nope = rmsnorm(kv[..., :MLA_NOPE], g_k_nope)
    v_mla = kv[..., MLA_NOPE:]
    o_mla = causal_block_attention((q_nope, q_pe), (k_nope, kpe_all), v_mla, pos, k_pos,
                                   (MLA_NOPE + MLA_ROPE) ** -0.5)
    c = jnp.cumsum(logf_all.astype(jnp.float32), axis=1)
    o_fox = causal_block_attention((fq,), (fk_all,), fv_all, pos, k_pos, FOX_DIM ** -0.5,
                                   c_q=c[:, n_past:], c_k=c)
    mixed = jnp.concatenate([rmsnorm(o_mla.reshape(B, T, MLA_HEADS * MLA_V), g_out_mla),
                             rmsnorm(o_fox.reshape(B, T, FOX_HEADS * FOX_DIM), g_out_fox)], axis=-1)
    out = jnp.einsum('bte,ed->btd', mixed, w_o)
    return out, (ckv, kpe, fk, fv, logf)

def peer_ffn(xn, w_peer_q, peer_sub_keys, peer_u, peer_v):
    B, T, D = xn.shape
    N = B * T
    n_blocks = -(-N // PEER_BLOCK)
    pad = n_blocks * PEER_BLOCK - N
    xf = jnp.pad(xn.reshape(N, D), ((0, pad), (0, 0))).reshape(n_blocks, PEER_BLOCK, D)

    def one_block(xb):
        q = jnp.einsum('td,de->te', xb, w_peer_q).reshape(PEER_BLOCK, PEER_HEADS, 2, PEER_DKEY // 2)
        s = jnp.einsum('thpc,hpkc->thpk', q, peer_sub_keys, preferred_element_type=jnp.float32)
        top_s, top_i = lax.top_k(s, PEER_TOPK)
        cand_s = (top_s[:, :, 0, :, None] + top_s[:, :, 1, None, :]).reshape(PEER_BLOCK, PEER_HEADS, PEER_TOPK * PEER_TOPK)
        cand_i = (top_i[:, :, 0, :, None] * PEER_KEYS + top_i[:, :, 1, None, :]).reshape(PEER_BLOCK, PEER_HEADS, PEER_TOPK * PEER_TOPK)
        best_s, best_pos = lax.top_k(cand_s, PEER_TOPK)
        expert = jnp.take_along_axis(cand_i, best_pos, axis=-1)
        gate = jax.nn.softmax(best_s, axis=-1)
        u = peer_u[expert]
        act = jax.nn.gelu(jnp.einsum('thkd,td->thk', u, xb, preferred_element_type=jnp.float32), approximate=False)
        return jnp.einsum('thk,thkd->td', (gate * act).astype(peer_v.dtype), peer_v[expert])

    y = lax.map(one_block, xf).reshape(n_blocks * PEER_BLOCK, D)[:N]
    return y.reshape(B, T, D).astype(xn.dtype)

def decoder_layer(x, past, g_attn, w_in, b_forget, g_q_nope, g_q_pe, g_ckv, g_k_pe, w_ukv, g_k_nope,
                  g_fox_q, g_fox_k, g_out_mla, g_out_fox, w_o, g_ffn, w_peer_q, peer_sub_keys, peer_u, peer_v):
    mix, rows = token_mixers(rmsnorm(x, g_attn), past, w_in, b_forget, g_q_nope, g_q_pe, g_ckv, g_k_pe,
                             w_ukv, g_k_nope, g_fox_q, g_fox_k, g_out_mla, g_out_fox, w_o)
    h = x + mix
    y = h + peer_ffn(rmsnorm(h, g_ffn), w_peer_q, peer_sub_keys, peer_u, peer_v)
    return y, rows

def setup_inputs(seed: int = 0) -> dict:
    key = jax.random.key(seed)
    k = jax.random.split(key, 32)
    f32 = jnp.float32

    def nrm(i, shape, scale):
        return scale * jax.random.normal(k[i], shape, f32)

    def gain(i, shape):
        return 1.0 + 0.1 * jax.random.normal(k[i], shape, f32)

    n_pages = PAST_LEN // PAGE_SIZE
    n_used = DEC_BATCH * n_pages
    n_pool = n_used + n_used // 4
    page_table = jax.random.permutation(k[7], n_pool)[:n_used].reshape(DEC_BATCH, n_pages).astype(jnp.int32)
    pool = (DEPTH, n_pool, PAGE_SIZE)
    return {
        'x_prompt': nrm(0, (BATCH, SEQ, D_MODEL), 1.0),
        'x_sample': nrm(1, (DEC_BATCH, DEC_SEQ, D_MODEL), 1.0),
        'cache_mla_latent': nrm(2, pool + (KV_RANK,), 1.0),
        'cache_mla_kpe': nrm(3, pool + (MLA_ROPE,), 1.0),
        'cache_fox_k': nrm(4, pool + (FOX_HEADS, FOX_DIM), 1.0),
        'cache_fox_v': nrm(5, pool + (FOX_HEADS, FOX_DIM), 1.0),
        'cache_fox_logf': jax.nn.log_sigmoid(3.0 + jax.random.normal(k[6], pool + (FOX_HEADS,), f32)),
        'page_table': page_table,
        'g_attn': gain(8, (DEPTH, D_MODEL)),
        'w_in': nrm(9, (DEPTH, D_MODEL, D_IN_PROJ), D_MODEL ** -0.5),
        'b_forget': jnp.linspace(1.0, 6.0, FOX_HEADS, dtype=f32)[None, :] + nrm(10, (DEPTH, FOX_HEADS), 0.1),
        'g_q_nope': gain(11, (DEPTH, MLA_NOPE)),
        'g_q_pe': gain(12, (DEPTH, MLA_ROPE)),
        'g_ckv': gain(13, (DEPTH, KV_RANK)),
        'g_k_pe': gain(14, (DEPTH, MLA_ROPE)),
        'w_ukv': nrm(15, (DEPTH, KV_RANK, MLA_HEADS * (MLA_NOPE + MLA_V)), KV_RANK ** -0.5),
        'g_k_nope': gain(16, (DEPTH, MLA_NOPE)),
        'g_fox_q': gain(17, (DEPTH, FOX_DIM)),
        'g_fox_k': gain(18, (DEPTH, FOX_DIM)),
        'g_out_mla': gain(19, (DEPTH, MLA_HEADS * MLA_V)),
        'g_out_fox': gain(20, (DEPTH, FOX_HEADS * FOX_DIM)),
        'w_o': nrm(21, (DEPTH, D_MIX, D_MODEL), D_MIX ** -0.5),
        'g_ffn': gain(22, (DEPTH, D_MODEL)),
        'w_peer_q': nrm(23, (DEPTH, D_MODEL, PEER_HEADS * PEER_DKEY), D_MODEL ** -0.5),
        'peer_sub_keys': nrm(24, (DEPTH, PEER_HEADS, 2, PEER_KEYS, PEER_DKEY // 2), (PEER_DKEY // 2) ** -0.5),
        'peer_u': nrm(25, (DEPTH, PEER_EXPERTS, D_MODEL), D_MODEL ** -0.5),
        'peer_v': nrm(26, (DEPTH, PEER_EXPERTS, D_MODEL), PEER_HEADS ** -0.5),
    }

def reference(x_prompt, x_sample, cache_mla_latent, cache_mla_kpe, cache_fox_k, cache_fox_v, cache_fox_logf,
              page_table, g_attn, w_in, b_forget, g_q_nope, g_q_pe, g_ckv, g_k_pe, w_ukv, g_k_nope,
              g_fox_q, g_fox_k, g_out_mla, g_out_fox, w_o, g_ffn, w_peer_q, peer_sub_keys, peer_u, peer_v):
    def gather(cache):
        g = cache[page_table]
        return g.reshape((g.shape[0], g.shape[1] * g.shape[2]) + g.shape[3:])

    y_prompt, y_sample = x_prompt, x_sample
    prompt_rows, sample_rows = [], []
    for l in range(DEPTH):
        lw = (g_attn[l], w_in[l], b_forget[l], g_q_nope[l], g_q_pe[l], g_ckv[l], g_k_pe[l], w_ukv[l],
              g_k_nope[l], g_fox_q[l], g_fox_k[l], g_out_mla[l], g_out_fox[l], w_o[l], g_ffn[l],
              w_peer_q[l], peer_sub_keys[l], peer_u[l], peer_v[l])
        y_prompt, rows_p = decoder_layer(y_prompt, None, *lw)
        past = (gather(cache_mla_latent[l]), gather(cache_mla_kpe[l]), gather(cache_fox_k[l]),
                gather(cache_fox_v[l]), gather(cache_fox_logf[l]))
        y_sample, rows_s = decoder_layer(y_sample, past, *lw)
        prompt_rows.append(rows_p)
        sample_rows.append(rows_s)
    lat_p, kpe_p, fk_p, fv_p, lf_p = [jnp.stack([r[i] for r in prompt_rows]) for i in range(5)]
    lat_s, kpe_s, fk_s, fv_s, lf_s = [jnp.stack([r[i] for r in sample_rows]) for i in range(5)]
    return (y_prompt, y_sample, lat_p, kpe_p, fk_p, fv_p, lf_p, lat_s, kpe_s, fk_s, fv_s, lf_s)


_drawn_inputs = setup_inputs


def setup_inputs(seed=0):
    import zlib

    import numpy as np

    out = dict(_drawn_inputs(seed))
    spreads = {}
    factors = {}
    for name, (base, spread) in spreads.items():
        noise = np.random.default_rng([zlib.crc32(name.encode()), seed]).standard_normal(out[name].shape)
        drawn = base * np.exp(spread * noise) if base else spread * noise
        out[name] = __import__('jax').numpy.asarray(drawn.astype(out[name].dtype))
    for name, factor in factors.items():
        out[name] = (out[name] * factor).astype(out[name].dtype)
    return out
```

```python
from contextlib import ExitStack

import numpy as np

import concourse.bass as bass
from concourse import mybir

ALU = mybir.AluOpType
ACT = mybir.ActivationFunctionType
AX = mybir.AxisListType
F32 = mybir.dt.float32
U32 = mybir.dt.uint32
I32 = mybir.dt.int32

P = 128
D = 1024
DC = D // P
T = 512
NB = T // P
BD = 8
PAST = 4096
PAGE = 128
NPG = PAST // PAGE
H = 8
NOPE = 64
RP = 32
VD = 64
R = 128
FD = 64
KM = NOPE + RP
KF = FD + 2
QW = H * (KM + KF)
WIN = 2472
PHEADS = 8
NHP = 2 * PHEADS
TOPK = 16
SLOTS = PHEADS * TOPK
EPS = 1e-6
S_MLA = float(KM) ** -0.5
S_FOX = float(FD) ** -0.5
NEG = -1e30
RING = 8
TAIL_QPE, TAIL_CKV, TAIL_KPE, TAIL_F = 0, 256, 384, 416
TAIL = 424
G_QN, G_QPE, G_CKV, G_KPE, G_KN, G_FQ, G_FK, G_BF = 0, 64, 96, 224, 256, 320, 384, 448
GS = 456
C_ID, C_MASK, C_TRI, C_ONES, C_COS, C_SIN, C_DIM, C_IOTA, C_END = 0, 128, 256, 384, 512, 592, 672, 706, 722
E_HM, E_BT, E_B, E_VE, E_PAR, E_MOD, E_END = 0, 256, 384, 392, 1416, 1418, 1420


def build(nc, x_prompt, x_sample, w_in, w_k, w_v, w_kT, w_o, w_q, sub_keys, gains, g_cols, g_ffn, consts, dec_consts,
          pages, page_rows, kt_pool, kpe_pool, vn_pool, logf_pool, peer_u, peer_v,
          y_prompt, y_sample, lat_p, kpe_p, fk_p, fv_p, lf_p, lat_s, kpe_s, fk_s, fv_s, lf_s):
    ctx = ExitStack()
    with ctx:
        def sb(name, shape, dt=F32):
            return ctx.enter_context(nc.sbuf_tensor(name, shape, dt))

        def sem(name):
            return ctx.enter_context(nc.semaphore(name))

        h_dram = nc.dram_tensor("h_scratch", (NB * P + BD, D), F32, kind="Internal").ap()
        qs_dram = nc.dram_tensor("q_scratch", (BD, QW), F32, kind="Internal").ap()
        ks_dram = nc.dram_tensor("k_scratch", (BD, QW), F32, kind="Internal").ap()
        vs_dram = nc.dram_tensor("v_scratch", (BD, H * FD), F32, kind="Internal").ap()
        cs_dram = nc.dram_tensor("c_scratch", (BD, R), F32, kind="Internal").ap()

        KB = 256
        arena = sb("arena", [P, 184 * KB])

        def part(kib, n):
            a = int(kib * KB)
            return arena[:, a:a + n]

        win = part(0, DC * WIN).rearrange("p (c n) -> p c n", c=DC)
        KT = part(77.5, 16 * T).rearrange("p (h t) -> p h t", h=16)
        V = part(109.5, NB * D).rearrange("p (b n) -> p b n", b=NB)
        QT = part(125.5, 16 * P).rearrange("p (h t) -> p h t", h=16)
        Qk = part(133.5, QW)
        Kk = part(133.5 + 5.0625, QW)
        mixT = part(144, NB * D).rearrange("p (b c t) -> p b c t", b=NB, c=DC)
        xn2 = part(144, NB * D).rearrange("p (b n) -> p b n", b=NB)
        sq = part(160, 2048)
        Pm = part(160, 1024).rearrange("p (i n) -> p i n", i=2)
        PT = part(164, 1024).rearrange("p (i n) -> p i n", i=2)
        mx = part(168, D)
        xnT = part(172, D).rearrange("p (c t) -> p c t", c=DC)
        wk = part(176, 512)
        wv = part(178, 512)
        pe9 = part(180, 288).rearrange("p (h d) -> p h d", h=9)
        rp9 = part(181.25, 288).rearrange("p (h d) -> p h d", h=9)
        rt = part(182.5, 288).rearrange("p (i h d) -> p i h d", i=2, h=9)
        wq = part(0, DC * 2048).rearrange("p (c n) -> p c n", c=DC)
        wo = part(64, DC * D).rearrange("p (c n) -> p c n", c=DC)
        qpT = part(128, NHP * P).rearrange("p (g t) -> p g t", g=NHP)
        skT = part(136, NHP * P).rearrange("p (g k) -> p g k", g=NHP)
        sc = part(160, 3 * NHP * P).rearrange("p (i g k) -> p i g k", i=3, g=NHP)
        ring = part(96, RING * D).rearrange("p (s n) -> p s n", s=RING)
        W32 = part(128, 4 * 32 * 32).rearrange("p (j c m) -> p j c m", j=4, c=32)
        SA = part(0, PAST)
        SB = part(16, PAST)
        SR = part(32, PAST)
        SABR = part(0, 3 * PAST).rearrange("p (k n) -> p k n", k=3)
        kbuf = part(48, 2 * 4 * 640).rearrange("p (i j n) -> p i j n", i=2, j=4)
        kpb = part(68, 2 * 4 * 128).rearrange("p (i j n) -> p i j n", i=2, j=4)
        sqd = part(72, 1024).rearrange("p (i n) -> p i n", i=2)
        pTd = part(76, 256).rearrange("p (i n) -> p i n", i=2)
        dcon = part(77, E_END)
        wkd = part(83, 512)
        wkTd = part(85, 512).rearrange("p (q r) -> p q r", q=4)
        qz = part(87, 5 * BD * 32).rearrange("p (c b m) -> p c b m", c=5, b=BD)
        qpz = part(92, BD * 32).rearrange("p (b m) -> p b m", b=BD)
        qTd = part(93, 8 * BD).rearrange("p (c b) -> p c b", c=8)
        qbd = part(93.25, 4 * 16).rearrange("p (q m) -> p q m", q=4)
        qpT8 = part(93.5, 8 * BD).rearrange("p (h b) -> p h b", h=8)
        dsm = part(94, 512)
        stg = part(93, 256).rearrange("p (i n) -> p i n", i=2)
        wo_s = part(16, DC * D).rearrange("p (c n) -> p c n", c=DC)
        WQ_S = [160, 168, 176, 0, 8, 48, 56, 144]
        wq_s = [part(k, 2048) for k in WQ_S]
        skT_s = part(152, 2048).rearrange("p (g k) -> p g k", g=NHP)
        oX = part(83, 512)
        oL = part(85, 128)
        oLT = part(85.5, 128)
        mxs = part(87, D)
        xTs = part(91, 64).rearrange("p (c t) -> p c t", c=DC)
        qTs = part(91.25, 128).rearrange("p (g t) -> p g t", g=NHP)
        wvs = part(68, 512)
        xs2 = part(64, D)[0:BD, :]
        selT = part(68, D)[0:BD, :].rearrange("p (t m) -> p t m", t=BD)
        oY = part(89, 512)
        pself = part(86, P)[0:BD, :]
        kscr = part(48, PAST)
        LG = part(168, PAST)
        lgf = dsm[:, 320:352]
        lgi = dsm[:, 352:384].bitcast(U32)
        prow = dsm[:, 384:416].bitcast(I32)
        Wd = W32[:, :, :, :].rearrange("p j c m -> p j (c m)")[:, :, 0:1024:33]
        QKB = [7, 0, 1, 2, 3, 4, 5, 6]
        hs = part(72, D)
        hb = sb("hb", [P, D])
        gf = sb("gf", [P, D])
        con = sb("con", [P, C_END])
        gs = sb("gs", [P, GS])
        gT = sb("gT", [P, 2 * DC])
        ssa = sb("ssa", [P, 4])
        ssv = sb("ssv", [P, 34])
        lnv = sb("lnv", [P, 34])
        r0v = sb("r0v", [P, 34])
        rv = sb("rv", [P, 34])
        tv = sb("tv", [P, 34])
        ckvn = sb("ckvn", [P, R])
        eidf = ckvn
        lf = sb("lf", [P, 5, H])
        fz = sb("fz", [P, 4, H])
        nmx = sb("nmx", [P, 16])
        rs = sb("rs", [P, 16])
        eidx = sb("eidx", [P, SLOTS], U32)
        idxT = sb("idxT", [P, P], U32)
        gate = sb("gate", [P, 2, SLOTS])
        acc = sb("acc", [P, SLOTS])
        ckvT = acc
        topv = sb("topv", [P, NHP, TOPK])
        topi = sb("topi", [P, NHP, TOPK], U32)
        topf = sb("topf", [P, NHP, TOPK])
        mrep = sb("mrep", [P, 256])
        oneh = mrep
        cand = topi[:, :, :].rearrange("p a b -> p (a b)").bitcast(F32)
        bpos = sb("bpos", [P, 3, TOPK], U32)
        bposf = sb("bposf", [P, 2, TOPK])
        isel = sb("isel", [P, 2, TOPK])
        ptab = sb("ptab", [1, BD * NPG], I32)

        ps = ctx.enter_context(nc.psum_tensor("ps", [P, 8, 512], F32))
        ident = con[:, C_ID:C_ID + P]

        const_in = sem("const_in")
        win_in = sem("win_in")
        wq_in = sem("wq_in")
        wo_in = sem("wo_in")
        sk_in = sem("sk_in")
        x_in = sem("x_in")
        h_in = sem("h_in")
        h_made = sem("h_made")
        h_stored = sem("h_stored")
        stored = sem("stored")
        rows_out = sem("rows_out")
        s_rows = sem("s_rows")
        sumsq = sem("sumsq")
        rms_in = sem("rms_in")
        rms_out = sem("rms_out")
        xn_done = sem("xn_done")
        tr_ps = sem("tr_ps")
        xnT_done = sem("xnT_done")
        proj_ps = sem("proj_ps")
        sq_done = sem("sq_done")
        ckv_done = sem("ckv_done")
        ckv_ps = sem("ckv_ps")
        ckvT_done = sem("ckvT_done")
        kv_ps = sem("kv_ps")
        v_done = sem("v_done")
        xnT2_done = sem("xnT2_done")
        fz_done = sem("fz_done")
        fexp_done = sem("fexp_done")
        lf_done = sem("lf_done")
        c_ps = sem("c_ps")
        rp_done = sem("rp_done")
        rp_copied = sem("rp_copied")
        qk_done = sem("qk_done")
        qk_ps = sem("qk_ps")
        qk_even = sem("qk_even")
        qk_odd = sem("qk_odd")
        s_ps = sem("s_ps")
        max_done = sem("max_done")
        exp_done = sem("exp_done")
        pT_ps = sem("pT_ps")
        pT_done = [sem("pT_done_even"), sem("pT_done_odd")]
        o_ps = sem("o_ps")
        mx_done = sem("mx_done")
        mixT_done = sem("mixT_done")
        op_ps = sem("op_ps")
        xn2_done = sem("xn2_done")
        q_ps = sem("q_ps")
        q_done = sem("q_done")
        sc_ps = sem("sc_ps")
        sc_done = sem("sc_done")
        gexp_in = sem("gexp_in")
        gexp_out = sem("gexp_out")
        top_done = sem("top_done")
        idx_ps = sem("idx_ps")
        idxT_done = sem("idxT_done")
        g = [sem(f"gathered{i}") for i in range(RING)]
        u_used = sem("u_used")
        v_used = sem("v_used")
        gelu_done = sem("gelu_done")
        w_done = sem("w_done")
        w_ps = sem("w_ps")
        W_done = sem("W_done")
        y_done = sem("y_done")
        a_tok = sem("a_tok")
        dm_done = sem("dm_done")
        s_mT = sem("s_mT")
        s_h = sem("s_h")
        s_gT = sem("s_gT")
        ssk_in = sem("ssk_in")
        gates_done = sem("gates_done")
        oL_done = sem("oL_done")
        oLT_ps = sem("oLT_ps")
        v_step = sem("v_step")
        a_step = sem("a_step")
        p_step = sem("p_step")
        l_step = sem("l_step")
        dec_in = sem("dec_in")
        k_in = [sem("k_in0"), sem("k_in1")]
        k_used = sem("k_used")
        n_ps = sem("n_ps")
        sqd_done = sem("sqd_done")
        sqd_used = sem("sqd_used")
        abr_done = sem("abr_done")
        dq_done = sem("dq_done")
        d_ps = sem("d_ps")
        stg_done = sem("stg_done")
        lg_gathered = sem("lg_gathered")
        dq_in = sem("dq_in")
        s_sum = sem("s_sum")
        s_op = sem("s_op")
        s_xn = sem("s_xn")
        s_tr = sem("s_tr")
        s_xT = sem("s_xT")
        s_q = sem("s_q")
        s_qT = sem("s_qT")
        s_sc = sem("s_sc")
        s_u = sem("s_u")
        s_xb = sem("s_xb")
        s_v = sem("s_v")
        selT_done = sem("selT_done")
        v_in = sem("v_in")
        sx_in = sem("sx_in")
        swo_in = sem("swo_in")
        swq_in = sem("swq_in")
        zeroed = sem("zeroed")
        d_sb = sem("d_sb")
        soft_in = sem("soft_in")
        soft_ln = sem("soft_ln")
        soft_max = sem("soft_max")
        soft_exp = sem("soft_exp")
        lg_in = sem("lg_in")
        pd_ps = sem("pd_ps")
        pd_done = sem("pd_done")

        block = ctx.enter_context(nc.Block())

        ROWS = [P] * NB + [BD]
        SBLK = NB
        def gcol(i):
            return 32 * (i % 4) + i // 4

        @block.sync
        def _(sp):
            sp.dma_start(con[:, :], consts).then_inc(const_in, 16)
            sp.dma_start(gs[:, :], gains.partition_broadcast(P)).then_inc(const_in, 16)
            sp.dma_start(gT[:, :], g_cols).then_inc(const_in, 16)
            sp.dma_start(hb[:, :], x_prompt[0:P, :]).then_inc(x_in, 16)
            for c in range(DC):
                sp.dma_start(win[:, c, :], w_in[:, c, :]).then_inc(win_in, 16)
            sp.dma_start(wk, w_k).then_inc(const_in, 16)
            sp.dma_start(wv, w_v).then_inc(const_in, 16)
            sp.dma_start(gf[:, :], g_ffn.partition_broadcast(P)).then_inc(const_in, 16)
            sp.dma_start(ptab[:, :], pages).then_inc(const_in, 16)
            for b in range(NB + 1):
                n = ROWS[b]
                if b + 1 <= NB:
                    sp.wait_ge(xn_done, 2 * b + 1)
                    nx = x_prompt[(b + 1) * P:(b + 2) * P, :] if b + 1 < NB else x_sample
                    sp.dma_start(hb[0:ROWS[b + 1], :], nx).then_inc(x_in, 16)
                outs = ([lat_p[b * P:(b + 1) * P], kpe_p[b * P:(b + 1) * P], fk_p[b * P:(b + 1) * P],
                         fv_p[b * P:(b + 1) * P], lf_p[b * P:(b + 1) * P]] if b < NB
                        else [lat_s, kpe_s, fk_s, fv_s, lf_s])
                vb = b if b < NB else 0
                sp.wait_ge(qk_done, b + 1)
                sp.wait_ge(v_done, 2 * (b + 1))
                sp.dma_start(outs[0], ckvn[0:n, :]).then_inc(rows_out, 16)
                sp.dma_start(outs[1], rp9[0:n, 8, :]).then_inc(rows_out, 16)
                kf = Kk[0:n, H * KM:].rearrange("p (h d) -> p h d", h=H)
                sp.dma_start(outs[2].rearrange("t (h d) -> t h d", h=H), kf[:, :, 0:FD]).then_inc(rows_out, 16)
                sp.dma_start(outs[3], V[0:n, vb, 512:1024]).then_inc(rows_out, 16)
                sp.dma_start(outs[4], lf[0:n, b, :]).then_inc(rows_out, 16)
                if b == SBLK:
                    sp.dma_start(qs_dram, Qk[0:n, :]).then_inc(s_rows, 16)
                    sp.dma_start(ks_dram, Kk[0:n, :]).then_inc(s_rows, 16)
                    sp.dma_start(vs_dram, V[0:n, 0, 512:1024]).then_inc(s_rows, 16)
                    sp.dma_start(cs_dram, ckvn[0:n, :]).then_inc(s_rows, 16)
            sp.wait_ge(mixT_done, NB)
            sp.wait_ge(rows_out, 80 * (NB + 1))
            sp.wait_ge(s_rows, 64)
            for c in range(DC):
                sp.dma_start(wo[:, c, :], w_o[:, c, :]).then_inc(wo_in, 16)
            for c in range(DC):
                sp.dma_start(wq[:, c, :], w_q[:, c, :]).then_inc(wq_in, 16)
            sp.dma_start(skT, sub_keys).then_inc(sk_in, 16)
            for b in range(NB):
                if b:
                    sp.wait_ge(q_ps, b)
                else:
                    sp.wait_ge(xn_done, 2 * NB + 1)
                sp.dma_start(hb[:, :], x_prompt[b * P:(b + 1) * P, :]).then_inc(x_in, 16)
                sp.wait_ge(h_made, b + 1)
                sp.dma_start(h_dram[b * P:(b + 1) * P, :], hb[:, :]).then_inc(h_stored, 16)
            sp.wait_ge(sc_done, NB)
            sp.dma_start(dcon, dec_consts).then_inc(dec_in, 16)
            sp.dma_start(wkd, w_k).then_inc(dec_in, 16)
            sp.dma_start(wkTd, w_kT).then_inc(dec_in, 16)
            sp.dma_start(SB[0:BD, 0:QW], qs_dram).then_inc(dec_in, 16)
            sp.dma_start(SA[0:BD, 0:QW], ks_dram).then_inc(dec_in, 16)
            sp.dma_start(prow, page_rows).then_inc(dec_in, 16)
            sp.wait_ge(const_in, 16 * 7)

            def load_unit(i, par, keys):
                for j in range(4):
                    pg = sp.value_load(ptab[0:1, bass.ds(i * 8 + (par * 4 + j), 1)], min_val=0,
                                       max_val=kt_pool.shape[0] - 1)
                    src = kt_pool if keys else vn_pool
                    sp.dma_start(kbuf[:, par, j, :], src[bass.ds(pg, 1), :, :]
                                 .rearrange("a p n -> p (a n)")).then_inc(k_in[par], 16)
                    if keys:
                        sp.dma_start(kpb[0:RP, par, j, :], kpe_pool[bass.ds(pg, 1), :, :]
                                     .rearrange("a p n -> p (a n)")).then_inc(k_in[par], 16)

            for par in range(2):
                load_unit(0, par, True)
            with sp.Fori(1, NPG) as i:
                for par in range(2):
                    sp.wait_ge(k_used, sp.snap(2 * i + (par - 1)))
                    sp.sem_inc(l_step, 1)
                    load_unit(i, par, True)
            sp.wait_ge(abr_done, NPG + 2)
            sp.dma_start(sqd[0:BD, 0, :], vs_dram).then_inc(v_in, 16)
            sp.dma_start(sqd[0:BD, 1, 0:R], cs_dram).then_inc(v_in, 16)
            sp.dma_start(wvs, w_v).then_inc(v_in, 16)
            sp.wait_ge(soft_exp, 1)
            with sp.Fori(0, NPG) as i:
                for par in range(2):
                    sp.wait_ge(k_used, sp.snap(2 * i + (2 * NPG + par - 1)))
                    sp.sem_inc(l_step, 1)
                    load_unit(i, par, False)
            for c in range(DC):
                sp.dma_start(wo_s[:, c, :], w_o[:, c, :]).then_inc(swo_in, 16)
            sp.wait_ge(u_used, P * NB)
            for c in (0, 1, 2, 7):
                sp.dma_start(wq_s[c], w_q[:, c, :]).then_inc(swq_in, 16)
            sp.dma_start(skT_s, sub_keys).then_inc(ssk_in, 16)
            sp.wait_ge(k_used, 4 * NPG)
            sp.dma_start(hs[0:BD, :], x_sample).then_inc(sx_in, 16)
            for c in (3, 4, 5, 6):
                sp.dma_start(wq_s[c], w_q[:, c, :]).then_inc(swq_in, 16)
            sp.wait_ge(rows_out, 80 * (NB + 1))
            sp.wait_ge(h_stored, 16 * NB)
            sp.wait_ge(stored, 16 * (NB + 1))

        @block.gpsimd
        def _(pool):
            def gather(table, index, q):
                pool.indirect_dma_start(ring[:, q % RING, :], None, table,
                                        bass.IndirectOffsetOnAxis(ap=index, axis=0)).then_inc(g[q % RING], 16)

            pool.wait_ge(rows_out, 80 * (NB + 1))
            pool.wait_ge(s_rows, 64)
            for b in range(NB):
                pool.wait_ge(top_done, b + 1)
                if b == 2:
                    pool.wait_ge(lg_in, 1)
                    for i in range(NPG):
                        pool.indirect_dma_start(LG[:, i * P:(i + 1) * P], None, logf_pool,
                                                bass.IndirectOffsetOnAxis(ap=lgi[:, i:i + 1], axis=0)
                                                ).then_inc(lg_gathered, 16)
                for k in range(SLOTS):
                    if k >= RING:
                        pool.wait_ge(u_used, P * b + k - RING + 1)
                    elif b:
                        pool.wait_ge(v_used, P * b + k - RING + 1)
                    gather(peer_u, eidx[:, k:k + 1], 2 * P * b + k)
                pool.wait_ge(idxT_done, b + 1)
                for k in range(P):
                    if k >= RING:
                        pool.wait_ge(v_used, P * b + k - RING + 1)
                    else:
                        pool.wait_ge(u_used, P * (b + 1) + k - RING + 1)
                    gather(peer_v, idxT[:, gcol(k):gcol(k) + 1], 2 * P * b + P + k)
            pool.wait_ge(idxT_done, NB + 1)
            for k in range(BD):
                pool.wait_ge(v_used, P * NB + k - RING + 1)
                gather(peer_u, idxT[:, k:k + 1], 2 * P * NB + k)
            for k in range(BD):
                pool.wait_ge(s_u, k + 1)
                gather(peer_v, idxT[:, k:k + 1], 2 * P * NB + BD + k)

        @block.scalar
        def _(act):
            steps = [0, 0, 0]

            def step(ins):
                steps[0] += 1
                ins.then_inc(a_step, 1)
                act.wait_ge(a_step, steps[0])

            def rms(n, k):
                steps[1] += 1
                act.wait_ge(rms_in, steps[1])
                step(nc.scalar.activation(lnv[0:n, 0:k], ssv[0:n, 0:k], ACT.Ln))
                nc.scalar.activation(r0v[0:n, 0:k], lnv[0:n, 0:k], ACT.Exp, scale=-0.5).then_inc(rms_out, 1)

            act.wait_ge(const_in, 16 * 7)
            for b in range(NB + 1):
                n = ROWS[b]
                vb = b if b < NB else 0
                act.wait_ge(x_in, 16 * (b + 1))
                if 0 < b:
                    act.wait_ge(mixT_done, b)
                nc.scalar.activation(sq[0:n, 0:D], hb[0:n, :], ACT.Square,
                                     accum_out=ssa[0:n, 0:1]).then_inc(sumsq, 1)
                rms(n, 1)
                for i, m in ((0, 512), (1, 512), (2, 512), (4, 416)):
                    act.wait_ge(proj_ps, 5 * b + i + 1)
                    if i == 0:
                        act.wait_ge(rms_out, steps[1])
                    o = min(i, 3) * 512
                    last = nc.scalar.activation(sq[0:n, o:o + m], ps[0:n, i, 0:m], ACT.Square)
                last.then_inc(sq_done, 1)
                if b == SBLK:
                    act.wait_ge(rows_out, 80 * b)
                nc.scalar.activation(V[0:n, vb, 512:1024], ps[0:n, 3, :], ACT.Copy).then_inc(v_done, 1)
                rms(n, 34)
                act.wait_ge(fz_done, b + 1)
                step(nc.scalar.activation(fz[0:n, 2, :], fz[0:n, 1, :], ACT.Exp, scale=-1.0))
                nc.scalar.activation(fz[0:n, 3, :], fz[0:n, 2, :], ACT.Ln, bias=1.0).then_inc(fexp_done, 1)
                act.wait_ge(ckv_ps, b + 1)
                nc.scalar.activation(ckvT[:, 0:n], ps[:, 7, 0:n], ACT.Copy).then_inc(ckvT_done, 1)
                act.wait_ge(kv_ps, b + 1)
                nc.scalar.activation(sq[0:n, 0:512], ps[0:n, 5, :], ACT.Square).then_inc(sq_done, 1)
                nc.scalar.activation(V[0:n, vb, 0:512], ps[0:n, 6, :], ACT.Copy).then_inc(v_done, 1)
                act.wait_ge(rp_done, b + 1)
                q3 = Qk[0:n, 0:H * KM].rearrange("p (h d) -> p h d", h=H)
                k3 = Kk[0:n, 0:H * KM].rearrange("p (h d) -> p h d", h=H)
                nc.scalar.activation(q3[:, :, NOPE:KM], rp9[0:n, 0:8, :], ACT.Copy)
                nc.scalar.activation(k3[:, :, NOPE:KM], rp9[0:n, 8:9, :].to_broadcast([n, H, RP]),
                                     ACT.Copy).then_inc(rp_copied, 1)
                rms(n, 8)
                if b == SBLK:
                    break
                for gi in range(0, 8, 2):
                    act.wait_ge(qk_ps, 8 * b + gi + 1)
                    kd = KM if gi % 4 < 2 else KF
                    src = ps[0:kd, QKB[gi], :].rearrange("p (h t) -> p h t", h=4)
                    h0 = 4 * (gi % 4)
                    dst = QT[0:kd, h0:h0 + 4, :] if gi < 4 else KT[0:kd, h0:h0 + 4, b * P:(b + 1) * P]
                    nc.scalar.activation(dst, src, ACT.Copy).then_inc(qk_even, 1)
                w = (b + 1) * P

                def copy_pT(hh):
                    act.wait_ge(pT_ps, 16 * b + hh + 1)
                    if 16 * b + hh >= 2:
                        act.wait_ge(o_ps, 16 * b + hh - 1)
                    nc.scalar.activation(PT[:, hh % 2, 0:w], ps[:, 4 + hh % 2, 0:w],
                                         ACT.Copy).then_inc(pT_done[1], 1)

                for hh in range(16):
                    act.wait_ge(max_done, 16 * b + hh + 1)
                    if 16 * b + hh >= 2:
                        act.wait_ge(pT_ps, 16 * b + hh - 1)
                    nc.scalar.activation(Pm[:, hh % 2, 0:w], ps[:, 2 + hh % 2, 0:w], ACT.Exp,
                                         bias=nmx[:, hh:hh + 1], accum_out=rs[:, hh:hh + 1]
                                         ).then_inc(exp_done, 1)
                    if hh and (hh - 1) % 2:
                        copy_pT(hh - 1)
                copy_pT(15)
                act.wait_ge(mx_done, b + 1)
                act.wait_ge(o_ps, 16 * (b + 1))
                for i in range(2):
                    last = nc.scalar.activation(sq[:, i * 512:(i + 1) * 512], mx[:, i * 512:(i + 1) * 512],
                                                ACT.Square, accum_out=ssa[:, 1 + i:2 + i])
                last.then_inc(sumsq, 1)
                rms(P, 2)

            def gate_exp(b):
                n = ROWS[b]
                act.wait_ge(gexp_in, b + 1)
                nc.scalar.activation(gate[0:n, b % 2, :], gate[0:n, b % 2, :], ACT.Exp).then_inc(gexp_out, 1)

            for b in range(NB):
                act.wait_ge(h_made, b + 1)
                nc.scalar.activation(xn2[:, b, :], hb[:, :], ACT.Square, accum_out=ssa[:, 3:4]).then_inc(sumsq, 1)
                rms(P, 1)
                act.wait_ge(tr_ps, NB + 1 + NB + b + 1)
                act.wait_ge(h_stored, 16 * (b + 1))
                for i in range(2):
                    last = nc.scalar.activation(hb[:, i * 512:(i + 1) * 512], ps[:, 6 + i, :], ACT.Copy)
                last.then_inc(xnT2_done, 1)
                if b == 1:
                    gate_exp(0)
                act.wait_ge(q_ps, b + 1)
                if b:
                    act.wait_ge(sc_ps, b)
                for i in range(4):
                    last = nc.scalar.activation(qpT[:, 4 * i:4 * i + 4, :], ps[:, 2 + i, :]
                                                .rearrange("p (g t) -> p g t", g=4), ACT.Copy)
                last.then_inc(q_done, 1)
                act.wait_ge(sc_ps, b + 1)
                if b == 3:
                    act.wait_ge(top_done, 1)
                for i, bank in enumerate((6, 7, 0, 1)):
                    last = nc.scalar.activation(sc[:, b % 3, 4 * i:4 * i + 4, :], ps[:, bank, :]
                                                .rearrange("p (g t) -> p g t", g=4), ACT.Copy)
                last.then_inc(sc_done, 1)

            act.wait_ge(dq_done, 1)
            act.wait_ge(d_ps, 1)
            nc.scalar.activation(qTd, ps[:, 6, 0:64].rearrange("p (c b) -> p c b", c=8), ACT.Copy)
            nc.scalar.activation(qpT8[0:RP], ps[0:RP, 6, 64:128].rearrange("p (c b) -> p c b", c=8),
                                 ACT.Copy).then_inc(d_sb, 1)
            act.sem_inc(sqd_done, 2)
            act.sem_inc(abr_done, 2)

            def gelu(b):
                act.wait_ge(u_used, P * (b + 1))
                nc.scalar.activation(acc[:, :], acc[:, :], ACT.Gelu).then_inc(gelu_done, 1)

            def load_h(b):
                if b:
                    act.wait_ge(stored, 16 * b)
                else:
                    act.wait_ge(q_ps, NB)
                act.dma_start(hb[:, :], h_dram[b * P:(b + 1) * P, :]).then_inc(h_in, 16)

            def store_y(b):
                act.wait_ge(y_done, b + 1)
                act.dma_start(y_prompt[b * P:(b + 1) * P, :], hb[:, :]).then_inc(stored, 16)

            def decode_scores(first, last_it):
                with act.Fori(first, last_it) as it:
                    for s in range(2):
                        for par in range(2):
                            for q in range(4):
                                m = (2 * s + par) * 4 + q
                                act.wait_ge(n_ps, act.snap(it * 16 + (m + 1)))
                                act.sem_inc(a_tok, 1)
                                act.wait_ge(sqd_used, act.snap(it * 16 + (m + 1)))
                                nc.scalar.activation(sqd[:, q % 2, :], ps[:, 2 + q % 2, :],
                                                     ACT.Square).then_inc(sqd_done, 1)
                        act.wait_ge(sqd_used, act.snap(it * 16 + (8 * s + 10)))
                        act.sem_inc(a_tok, 1)
                        nc.scalar.activation(SABR[:, :, bass.ds(it * 256 + s * 128, 128)],
                                             ps[:, 4 + s, 0:3 * P].rearrange("p (k n) -> p k n", k=3),
                                             ACT.Copy).then_inc(abr_done, 1)

            gelu(0)
            load_h(0)
            gate_exp(1)
            store_y(0)
            decode_scores(0, 8)
            gelu(1)
            load_h(1)
            gate_exp(2)
            store_y(1)
            decode_scores(8, 16)
            gelu(2)
            load_h(2)
            gate_exp(3)
            act.wait_ge(soft_in, 1)
            step(nc.scalar.activation(kscr, SR, ACT.Ln))
            nc.scalar.activation(kscr, kscr, ACT.Exp, scale=-0.5).then_inc(soft_ln, 1)
            act.wait_ge(soft_max, 1)
            nc.scalar.activation(SA, SA, ACT.Exp, bias=dsm[:, 34:35], accum_out=dsm[:, 36:37])
            nc.scalar.activation(dsm[:, 35:36], dsm[:, 32:33], ACT.Exp, bias=dsm[:, 34:35]).then_inc(soft_exp, 1)
            store_y(2)
            act.sem_inc(pd_done, 2)
            with act.Fori(0, NPG // 2) as it:
                for s in range(2):
                    act.wait_ge(pd_ps, act.snap(it * 2 + (s + 2)))
                    act.sem_inc(a_tok, 1)
                    nc.scalar.activation(stg[:, s, :], SA[:, bass.ds(it * 256 + s * 128, 128)],
                                         ACT.Copy).then_inc(stg_done, 1)
                    act.wait_ge(pd_ps, act.snap(it * 2 + (s + 4)))
                    act.sem_inc(a_tok, 1)
                    act.wait_ge(k_used, act.snap(it * 4 + (2 * NPG - 2 + 2 * s)))
                    nc.scalar.activation(pTd[:, s, :], ps[:, 2 + s, 0:P],
                                         ACT.Copy).then_inc(pd_done, 1)
            gelu(3)
            load_h(3)
            act.wait_ge(oLT_ps, 1)
            nc.scalar.activation(oLT, ps[:, 7, 0:P], ACT.Copy).then_inc(s_sum, 1)
            act.wait_ge(dm_done, 1)
            step(nc.scalar.activation(oX[0:BD, 0:512], mxs[0:BD, 0:512], ACT.Square, accum_out=ssa[0:BD, 1:2]))
            nc.scalar.activation(oX[0:BD, 0:512], mxs[0:BD, 512:1024], ACT.Square,
                                 accum_out=ssa[0:BD, 2:3]).then_inc(sumsq, 1)
            rms(BD, 2)
            act.wait_ge(s_h, 1)
            nc.scalar.activation(mxs[0:BD, :], hs[0:BD, :], ACT.Square, accum_out=ssa[0:BD, 3:4]).then_inc(sumsq, 1)
            rms(BD, 1)
            act.wait_ge(s_tr, 2)
            nc.scalar.activation(xTs, ps[:, 7, 0:64].rearrange("p (c t) -> p c t", c=DC), ACT.Copy).then_inc(s_xT, 1)
            act.wait_ge(s_q, 1)
            nc.scalar.activation(qTs, ps[:, 6, 0:128].rearrange("p (c t) -> p c t", c=NHP), ACT.Copy).then_inc(s_qT, 1)
            gate_exp(4)
            store_y(3)
            act.wait_ge(s_u, BD)
            nc.scalar.activation(acc[:, 0:BD], acc[:, 0:BD], ACT.Gelu).then_inc(gelu_done, 1)
            act.wait_ge(y_done, NB + 1)
            act.dma_start(y_sample, hs[0:BD, :]).then_inc(stored, 16)

        @block.vector
        def _(dve):
            count = {"step": 0, "rms": 0, "ssq": 0, "sq": 0}
            V_ = nc.vector

            def step(ins):
                count["step"] += 1
                ins.then_inc(v_step, 1)
                dve.wait_ge(v_step, count["step"])

            def rms(n, k):
                count["rms"] += 1
                dve.wait_ge(rms_out, count["rms"])
                step(V_.tensor_tensor(tv[0:n, 0:k], r0v[0:n, 0:k], r0v[0:n, 0:k], ALU.mult))
                step(V_.tensor_tensor(tv[0:n, 0:k], tv[0:n, 0:k], ssv[0:n, 0:k], ALU.mult))
                step(V_.tensor_scalar(tv[0:n, 0:k], tv[0:n, 0:k], -0.5, 1.5, ALU.mult, ALU.add))
                step(V_.tensor_tensor(rv[0:n, 0:k], tv[0:n, 0:k], r0v[0:n, 0:k], ALU.mult))

            def rms_of(n, src, dim):
                count["ssq"] += 1
                dve.wait_ge(sumsq, count["ssq"])
                V_.tensor_scalar(ssv[0:n, 0:src.shape[1]], src, 1.0 / dim, EPS, ALU.mult, ALU.add).then_inc(rms_in, 1)
                rms(n, src.shape[1])

            def heads(ap, n, h=H):
                return ap.rearrange("p (h d) -> p h d", h=h)

            def bc(ap, n, h, d):
                return ap.unsqueeze(2).to_broadcast([n, h, d])

            def gb(a, n, h, d):
                return gs[0:n, a:a + d].unsqueeze(1).to_broadcast([n, h, d])

            dve.wait_ge(const_in, 16 * 7)
            q3f = Qk[:, H * KM:].rearrange("p (h d) -> p h d", h=H)
            k3f = Kk[:, H * KM:].rearrange("p (h d) -> p h d", h=H)
            V_.memset(q3f[:, :, FD:FD + 1], 1.0)
            step(V_.memset(k3f[:, :, FD + 1:FD + 2], 1.0))

            for b in range(NB + 1):
                n = ROWS[b]
                rms_of(n, ssa[0:n, 0:1], D)
                V_.tensor_scalar(mx[0:n, :], hb[0:n, :], rv[0:n, 0:1], None, ALU.mult).then_inc(xn_done, 1)
                dve.wait_ge(tr_ps, (b + 1) + min(b, NB))
                for i in range(2):
                    last = V_.tensor_tensor(xnT[:, 4 * i:4 * i + 4, 0:n],
                                            ps[:, 5 + i, 0:4 * n].rearrange("p (c t) -> p c t", c=4),
                                            gT[:, 4 * i:4 * i + 4].unsqueeze(2).to_broadcast([P, 4, n]), ALU.mult)
                last.then_inc(xnT_done, 1)
                count["sq"] += 1
                dve.wait_ge(sq_done, count["sq"])
                for i in range(3):
                    V_.tensor_reduce(ssv[0:n, 8 * i:8 * i + 8], heads(sq[0:n, 512 * i:512 * i + 512], n),
                                     AX.X, ALU.add)
                V_.tensor_reduce(ssv[0:n, 24:32], heads(sq[0:n, 1536:1792], n), AX.X, ALU.add)
                V_.tensor_reduce(ssv[0:n, 32:33], sq[0:n, 1792:1920], AX.X, ALU.add)
                step(V_.tensor_reduce(ssv[0:n, 33:34], sq[0:n, 1920:1952], AX.X, ALU.add))
                step(V_.tensor_tensor(ssv[0:n, :], ssv[0:n, :], con[0:n, C_DIM:C_DIM + 34], ALU.mult))
                V_.tensor_scalar(ssv[0:n, :], ssv[0:n, :], EPS, None, ALU.add).then_inc(rms_in, 1)
                step(V_.tensor_tensor(fz[0:n, 0, :], ps[0:n, 4, TAIL_F:TAIL], gs[0:n, G_BF:G_BF + H], ALU.add))
                V_.scalar_tensor_tensor(fz[0:n, 1, :], fz[0:n, 0, :], -1.0, fz[0:n, 0, :], ALU.mult,
                                        ALU.max).then_inc(fz_done, 1)
                rms(n, 34)
                if b:
                    dve.wait_ge(rows_out, 80 * b)
                V_.scalar_tensor_tensor(ckvn[0:n, :], ps[0:n, 4, TAIL_CKV:TAIL_KPE], rv[0:n, 32:33],
                                        gs[0:n, G_CKV:G_CKV + R], ALU.mult, ALU.mult).then_inc(ckv_done, 1)
                V_.tensor_scalar(rv[0:n, 0:8], rv[0:n, 0:8], S_MLA, None, ALU.mult)
                V_.tensor_scalar(rv[0:n, 8:16], rv[0:n, 8:16], S_FOX, None, ALU.mult)
                step(V_.tensor_scalar(rv[0:n, 24:32], rv[0:n, 24:32], S_MLA, None, ALU.mult))
                q3 = heads(Qk[0:n, 0:H * KM], n)
                k3 = heads(Kk[0:n, 0:H * KM], n)
                V_.tensor_tensor(pe9[0:n, 0:8, :], heads(ps[0:n, 4, 0:256], n), bc(rv[0:n, 24:32], n, H, RP), ALU.mult)
                V_.tensor_scalar(pe9[0:n, 8, :], ps[0:n, 4, TAIL_KPE:TAIL_F], rv[0:n, 33:34], None, ALU.mult)
                V_.tensor_tensor(q3[:, :, 0:NOPE], heads(ps[0:n, 0, :], n), bc(rv[0:n, 0:8], n, H, NOPE), ALU.mult)
                V_.tensor_tensor(q3f[0:n, :, 0:FD], heads(ps[0:n, 1, :], n), bc(rv[0:n, 8:16], n, H, FD), ALU.mult)
                step(V_.tensor_tensor(k3f[0:n, :, 0:FD], heads(ps[0:n, 2, :], n), bc(rv[0:n, 16:24], n, H, FD), ALU.mult))
                V_.tensor_tensor(pe9[0:n, 0:8, :], pe9[0:n, 0:8, :], gb(G_QPE, n, H, RP), ALU.mult)
                V_.tensor_tensor(pe9[0:n, 8, :], pe9[0:n, 8, :], gs[0:n, G_KPE:G_KPE + RP], ALU.mult)
                V_.tensor_tensor(q3[:, :, 0:NOPE], q3[:, :, 0:NOPE], gb(G_QN, n, H, NOPE), ALU.mult)
                V_.tensor_tensor(q3f[0:n, :, 0:FD], q3f[0:n, :, 0:FD], gb(G_FQ, n, H, FD), ALU.mult)
                step(V_.tensor_tensor(k3f[0:n, :, 0:FD], k3f[0:n, :, 0:FD], gb(G_FK, n, H, FD), ALU.mult))
                cos = con[0:n, C_COS + 16 * b:C_COS + 16 * b + 16].unsqueeze(1).to_broadcast([n, 9, 16])
                sin = con[0:n, C_SIN + 16 * b:C_SIN + 16 * b + 16].unsqueeze(1).to_broadcast([n, 9, 16])
                x1, x2 = pe9[0:n, :, 0:16], pe9[0:n, :, 16:32]
                V_.tensor_tensor(rt[0:n, 0], x1, cos, ALU.mult)
                step(V_.tensor_tensor(rt[0:n, 1], x2, sin, ALU.mult))
                step(V_.tensor_tensor(rp9[0:n, :, 0:16], rt[0:n, 0], rt[0:n, 1], ALU.subtract))
                V_.tensor_tensor(rt[0:n, 0], x1, sin, ALU.mult)
                step(V_.tensor_tensor(rt[0:n, 1], x2, cos, ALU.mult))
                V_.tensor_tensor(rp9[0:n, :, 16:32], rt[0:n, 0], rt[0:n, 1], ALU.add).then_inc(rp_done, 1)
                dve.wait_ge(fexp_done, b + 1)
                V_.scalar_tensor_tensor(lf[0:n, b, :], fz[0:n, 0, :], 0.0, fz[0:n, 3, :], ALU.min,
                                        ALU.subtract).then_inc(lf_done, 1)
                count["sq"] += 1
                dve.wait_ge(sq_done, count["sq"])
                step(V_.tensor_reduce(ssv[0:n, 0:8], heads(sq[0:n, 0:512], n), AX.X, ALU.add))
                V_.tensor_scalar(ssv[0:n, 0:8], ssv[0:n, 0:8], 1.0 / NOPE, EPS, ALU.mult, ALU.add).then_inc(rms_in, 1)
                rms(n, 8)
                step(V_.tensor_tensor(k3[:, :, 0:NOPE], heads(ps[0:n, 5, :], n), bc(rv[0:n, 0:8], n, H, NOPE), ALU.mult))
                step(V_.tensor_tensor(k3[:, :, 0:NOPE], k3[:, :, 0:NOPE], gb(G_KN, n, H, NOPE), ALU.mult))
                if b == SBLK:
                    dve.wait_ge(rp_copied, b + 1)
                    V_.memset(q3f[0:n, :, FD + 1:FD + 2], 0.0)
                    V_.memset(k3f[0:n, :, FD:FD + 1], 0.0).then_inc(qk_done, 1)
                    break
                dve.wait_ge(c_ps, b + 1)
                cc = ps[:, 7, 256:256 + H].unsqueeze(2)
                V_.tensor_copy(q3f[:, :, FD + 1:FD + 2], cc)
                dve.wait_ge(rp_copied, b + 1)
                V_.tensor_scalar(k3f[:, :, FD:FD + 1], cc, -1.0, None, ALU.mult).then_inc(qk_done, 1)
                for gi in range(1, 8, 2):
                    dve.wait_ge(qk_ps, 8 * b + gi + 1)
                    kd = KM if gi % 4 < 2 else KF
                    src = ps[0:kd, QKB[gi], :].rearrange("p (h t) -> p h t", h=4)
                    h0 = 4 * (gi % 4)
                    dst = QT[0:kd, h0:h0 + 4, :] if gi < 4 else KT[0:kd, h0:h0 + 4, b * P:(b + 1) * P]
                    V_.tensor_copy(dst, src).then_inc(qk_odd, 1)
                w = (b + 1) * P

                def copy_pT(hh):
                    dve.wait_ge(pT_ps, 16 * b + hh + 1)
                    if 16 * b + hh >= 2:
                        dve.wait_ge(o_ps, 16 * b + hh - 1)
                    V_.tensor_copy(PT[:, hh % 2, 0:w], ps[:, 4 + hh % 2, 0:w]).then_inc(pT_done[0], 1)

                for hh in range(16):
                    dve.wait_ge(s_ps, 16 * b + hh + 1)
                    step(V_.tensor_tensor(ps[:, 2 + hh % 2, b * P:w], ps[:, 2 + hh % 2, b * P:w],
                                          con[:, C_MASK:C_MASK + P], ALU.add))
                    V_.tensor_reduce(nmx[:, hh:hh + 1], ps[:, 2 + hh % 2, 0:w], AX.X, ALU.max,
                                     negate=True).then_inc(max_done, 1)
                    if hh and (hh - 1) % 2 == 0:
                        copy_pT(hh - 1)
                dve.wait_ge(o_ps, 16 * (b + 1))
                step(V_.reciprocal(rs[:, :], rs[:, :]))
                V_.tensor_tensor(heads(mx[:, 0:512], P), heads(ps[:, 0, :], P), bc(rs[:, 0:8], P, H, VD), ALU.mult)
                V_.tensor_tensor(heads(mx[:, 512:1024], P), heads(ps[:, 1, :], P), bc(rs[:, 8:16], P, H, VD),
                                 ALU.mult).then_inc(mx_done, 1)
                rms_of(P, ssa[:, 1:3], 512)
                V_.tensor_scalar(mx[:, 0:512], mx[:, 0:512], rv[:, 0:1], None, ALU.mult)
                V_.tensor_scalar(mx[:, 512:1024], mx[:, 512:1024], rv[:, 1:2], None, ALU.mult).then_inc(xn_done, 1)
                dve.wait_ge(tr_ps, 2 * (b + 1))
                for i in range(2):
                    last = V_.tensor_tensor(mixT[:, b, 4 * i:4 * i + 4, :],
                                            ps[:, 6 + i, :].rearrange("p (c t) -> p c t", c=4),
                                            gT[:, DC + 4 * i:DC + 4 * i + 4].unsqueeze(2).to_broadcast([P, 4, P]),
                                            ALU.mult)
                last.then_inc(mixT_done, 1)

            def norm2(b):
                dve.wait_ge(op_ps, b + 1)
                dve.wait_ge(x_in, 16 * (NB + 1 + b + 1))
                for i in range(2):
                    last = V_.tensor_tensor(hb[:, i * 512:(i + 1) * 512], ps[:, i, :],
                                            hb[:, i * 512:(i + 1) * 512], ALU.add)
                last.then_inc(h_made, 1)
                rms_of(P, ssa[:, 3:4], D)
                V_.scalar_tensor_tensor(xn2[:, b, :], hb[:, :], rv[:, 0:1], gf[:, :], ALU.mult,
                                        ALU.mult).then_inc(xn2_done, 1)

            def top16(vals, pos, src, n, w):
                step(V_.max(vals[:, 0:8], src))
                V_.max_index(pos[:, 0:8], vals[:, 0:8], src)
                step(V_.match_replace(mrep[0:n, 0:w], vals[:, 0:8], src, NEG))
                step(V_.max(vals[:, 8:16], mrep[0:n, 0:w]))
                step(V_.max_index(pos[:, 8:16], vals[:, 8:16], mrep[0:n, 0:w]))

            def top_subkeys(b, scores, lo, hi):
                n = ROWS[b]
                for hp in range(lo, hi):
                    top16(topv[0:n, hp, :], topi[0:n, hp, :], scores(hp), n, P)

            def top_experts(b):
                n = ROWS[b]
                if b:
                    dve.wait_ge(idx_ps, b)
                step(V_.tensor_copy(topf[0:n], topi[0:n]))
                iota = con[0:n, C_IOTA:C_IOTA + 16].unsqueeze(1).to_broadcast([n, 16, 16])
                for h in range(PHEADS):
                    c3 = cand[0:n, :].rearrange("p (a b) -> p a b", a=16)
                    step(V_.tensor_tensor(c3, topv[0:n, 2 * h, :].unsqueeze(2).to_broadcast([n, 16, 16]),
                                          topv[0:n, 2 * h + 1, :].unsqueeze(1).to_broadcast([n, 16, 16]), ALU.add))
                    top16(gate[0:n, b % 2, 16 * h:16 * h + 16], bpos[0:n, 0, :], cand[0:n, :], n, 256)
                    V_.tensor_scalar(bpos[0:n, 1, :], bpos[0:n, 0, :], 4, None, ALU.logical_shift_right)
                    step(V_.tensor_scalar(bpos[0:n, 2, :], bpos[0:n, 0, :], 15, None, ALU.bitwise_and))
                    step(V_.tensor_copy(bposf[0:n, :, :], bpos[0:n, 1:3, :]))
                    o3 = oneh[0:n, :].rearrange("p (k a) -> p k a", a=16)
                    for i in range(2):
                        step(V_.tensor_tensor(o3, bposf[0:n, i, :].unsqueeze(2).to_broadcast([n, 16, 16]), iota,
                                              ALU.is_equal))
                        step(V_.tensor_tensor(o3, o3, topf[0:n, 2 * h + i, :].unsqueeze(1)
                                              .to_broadcast([n, 16, 16]), ALU.mult))
                        step(V_.tensor_reduce(isel[0:n, i, :], o3, AX.X, ALU.add))
                    step(V_.scalar_tensor_tensor(eidf[0:n, 16 * h:16 * h + 16], isel[0:n, 0, :], 128.0,
                                                 isel[0:n, 1, :], ALU.mult, ALU.add))
                V_.tensor_copy(eidx[0:n, :], eidf[0:n, :]).then_inc(top_done, 1)
                g3 = gate[0:n, b % 2, :].rearrange("p (h k) -> p h k", h=PHEADS)
                step(V_.tensor_copy(fz[0:n, 0, :].unsqueeze(2), g3[:, :, 0:1]))
                V_.tensor_tensor(g3, g3, bc(fz[0:n, 0, :], n, PHEADS, TOPK), ALU.subtract).then_inc(gexp_in, 1)
                dve.wait_ge(gexp_out, b + 1)
                step(V_.tensor_reduce(fz[0:n, 1, :], g3, AX.X, ALU.add))
                step(V_.reciprocal(fz[0:n, 2, :], fz[0:n, 1, :]))
                V_.tensor_tensor(g3, g3, bc(fz[0:n, 2, :], n, PHEADS, TOPK), ALU.mult).then_inc(gates_done, 1)
                dve.wait_ge(gates_done, b + 1)

            def scores_of(b):
                return lambda hp: sc[:, b % 3, hp, :]

            def copy_idxT(b):
                n = ROWS[b]
                dve.wait_ge(idx_ps, b + 1)
                V_.tensor_copy(idxT[:, 0:n], ps[:, 7, 0:n]).then_inc(idxT_done, 1)

            def decode_queries_1():
                dve.wait_ge(dec_in, 96)
                sc1 = SR[0:BD, 0:16 * KM]
                m3 = heads(sc1[:, 0:H * KM], BD)
                f3 = heads(sc1[:, H * KM:H * KM + 512], BD)
                qm, km = heads(SB[0:BD, 0:H * KM], BD), heads(SA[0:BD, 0:H * KM], BD)
                qf, kf = heads(SB[0:BD, H * KM:QW], BD), heads(SA[0:BD, H * KM:QW], BD)
                V_.tensor_tensor(m3, qm, km, ALU.mult)
                step(V_.tensor_tensor(f3, qf[:, :, 0:FD], kf[:, :, 0:FD], ALU.mult))
                V_.tensor_reduce(dsm[0:BD, 8:16], m3, AX.X, ALU.add)
                V_.tensor_reduce(dsm[0:BD, 0:8], f3, AX.X, ALU.add)
                V_.tensor_copy(dsm[0:BD, 16:24], lf[0:BD, SBLK, :])
                V_.memset(dsm[0:BD, 24:32], 0.0)
                V_.tensor_copy(heads(SR[0:BD, 2048:2560], BD), qf[:, :, 0:FD])
                V_.tensor_tensor(heads(SR[0:BD, 2560:3072], BD), qm[:, :, 0:NOPE], gb(G_KN, BD, H, NOPE), ALU.mult)
                V_.memset(qz, 0.0)
                V_.memset(qpz, 0.0)
                V_.memset(qbd, 0.0).then_inc(dq_done, 1)
                dve.wait_ge(dq_done, 1)
                for i in range(2):
                    m = dsm[0:BD, 64 + 128 * i:192 + 128 * i].rearrange("p (b r) -> p b r", b=BD)
                    last = V_.tensor_tensor(m, dcon[0:BD, E_BT:E_BT + P].rearrange("p (b r) -> p b r", b=BD),
                                            dsm[0:BD, 16 * i:16 * i + 16].unsqueeze(1).to_broadcast([BD, BD, 16]),
                                            ALU.mult)
                last.then_inc(dq_in, 1)

            def decode_queries_2():
                dve.wait_ge(d_sb, 1)
                for half in range(2):
                    hs_ = slice(64 * half, 64 * half + 64)
                    last = V_.tensor_copy(qbd[hs_, :, 8 * half:8 * half + 8], qTd[hs_, 4:8, :])
                last.then_inc(dq_in, 1)
                for half in range(2):
                    hs_ = slice(64 * half, 64 * half + 64)
                    for p2 in range(2):
                        for c in range(4):
                            m = 16 * p2 + 2 * c + half
                            V_.tensor_copy(qz[hs_, c, p2::2, m:m + 1], qTd[hs_, c, p2::2].unsqueeze(2))
                for p2 in range(2):
                    V_.tensor_copy(qpz[0:RP, p2::2, 16 * p2 + 8:16 * p2 + 16],
                                   qpT8[0:RP, :, p2::2].rearrange("p h j -> p j h"))
                dve.wait_ge(d_ps, 2)
                V_.tensor_copy(dsm[:, 32:34], ps[:, 6, 128:130])
                for q in range(4):
                    for half in range(2):
                        for p2 in range(2):
                            m = 16 * p2 + 8 + 2 * q + half
                            a = 256 + 16 * q + 8 * half
                            last = V_.tensor_copy(qz[:, 4, p2::2, m:m + 1],
                                                  ps[:, 6, a + p2:a + 8:2].unsqueeze(2))
                last.then_inc(dq_done, 1)

            def u_phase(b, between):
                for k in range(SLOTS):
                    if k % 8 == 0 and k // 8 in between:
                        for f in between[k // 8]:
                            f()
                    q = 2 * P * b + k
                    dve.wait_ge(g[q % RING], 16 * (q // RING + 1))
                    V_.tensor_tensor_reduce(ring[:, q % RING, :], ring[:, q % RING, :], xn2[:, b, :], 1.0, 0.0,
                                            ALU.mult, ALU.add, acc[:, k:k + 1]).then_inc(u_used, 1)
                dve.wait_ge(gelu_done, b + 1)
                V_.tensor_tensor(acc[:, :], acc[:, :], gate[:, b % 2, :], ALU.mult).then_inc(w_done, 1)
                dve.wait_ge(w_ps, b + 1)
                if b:
                    dve.wait_ge(v_used, P * b)
                V_.tensor_copy(Wd, ps[:, 7, 0:P].rearrange("p (j c) -> p j c", j=4)).then_inc(W_done, 1)

            def add_y(b):
                dve.wait_ge(v_used, P * (b + 1))
                dve.wait_ge(h_in, 16 * (b + 1))
                for i in range(2):
                    last = V_.tensor_tensor(hb[:, i * 512:(i + 1) * 512], ps[:, i, :],
                                            hb[:, i * 512:(i + 1) * 512], ALU.add)
                last.then_inc(y_done, 1)

            def zero_W():
                dve.wait_ge(sc_ps, NB)
                step(V_.memset(W32[:, :, :, :].rearrange("p j c m -> p (j c m)"), 0.0))

            norm2(0)
            dve.wait_ge(sc_done, 1)
            top_subkeys(0, scores_of(0), 0, 8)
            norm2(1)
            top_subkeys(0, scores_of(0), 8, 16)
            top_experts(0)
            norm2(2)
            u_phase(0, {4: [lambda: norm2(3)], 11: [lambda: copy_idxT(0), zero_W], 13: [decode_queries_1],
                        15: [decode_queries_2]})
            top_subkeys(1, scores_of(1), 0, 16)
            top_experts(1)
            u_phase(1, {1: [lambda: add_y(0)], 2: [lambda: copy_idxT(1)]})
            top_subkeys(2, scores_of(2), 0, 16)
            top_experts(2)
            step(V_.tensor_copy(lgf, prow))
            step(V_.tensor_scalar(lgf, lgf, 16.0, dcon[:, E_MOD:E_MOD + 1], ALU.mult, ALU.add))
            V_.tensor_copy(lgi, lgf).then_inc(lg_in, 1)
            u_phase(2, {1: [lambda: add_y(1)], 2: [lambda: copy_idxT(2)]})
            top_subkeys(3, scores_of(3), 0, 16)
            top_experts(3)
            dve.wait_ge(abr_done, NPG + 2)
            V_.tensor_scalar(SR, SR, 1.0 / NOPE, EPS, ALU.mult, ALU.add).then_inc(soft_in, 1)
            dve.wait_ge(soft_ln, 1)
            V_.tensor_tensor(SB, SB, kscr, ALU.mult)
            step(V_.tensor_tensor(SR, SR, kscr, ALU.mult))
            step(V_.tensor_tensor(SR, SR, kscr, ALU.mult))
            step(V_.tensor_scalar(SR, SR, -0.5, 1.5, ALU.mult, ALU.add))
            step(V_.tensor_tensor(SB, SB, SR, ALU.mult))
            step(V_.tensor_tensor(SA, SA, SB, ALU.add))
            dve.wait_ge(lg_gathered, 16 * NPG)
            step(V_.tensor_tensor_scan(SB, con[:, C_ONES:C_ONES + 1].to_broadcast([P, PAST]), LG, 0.0,
                                       ALU.mult, ALU.add))
            step(V_.tensor_tensor(dsm[:, 37:38], SB[:, PAST - 1:PAST], dsm[:, 33:34], ALU.add))
            step(V_.tensor_scalar(SB, SB, dsm[:, 37:38], -1.0, ALU.subtract, ALU.mult))
            step(V_.tensor_tensor(SA, SA, SB, ALU.add))
            step(V_.tensor_reduce(dsm[:, 38:39], SA, AX.X, ALU.max))
            step(V_.tensor_tensor(dsm[:, 38:39], dsm[:, 38:39], dsm[:, 32:33], ALU.max))
            V_.tensor_scalar(dsm[:, 34:35], dsm[:, 38:39], -1.0, None, ALU.mult).then_inc(soft_max, 1)
            dve.wait_ge(soft_exp, 1)
            V_.tensor_scalar(dsm[:, 48:56], dcon[:, E_B:E_B + BD], dsm[:, 35:36], None, ALU.mult).then_inc(dq_done, 1)
            step(V_.tensor_tensor(dsm[:, 39:40], dsm[:, 36:37], dsm[:, 35:36], ALU.add))
            step(V_.reciprocal(dsm[:, 40:41], dsm[:, 39:40]))
            V_.tensor_tensor(dsm[:, 41:42], dsm[:, 40:41], dcon[:, E_PAR:E_PAR + 1], ALU.mult)
            step(V_.tensor_tensor(dsm[:, 42:43], dsm[:, 40:41], dcon[:, E_PAR + 1:E_PAR + 2], ALU.mult))
            dve.wait_ge(pd_ps, 3)
            V_.tensor_copy(pself, ps[0:BD, 2, 256:384]).then_inc(dq_done, 1)
            u_phase(3, {1: [lambda: add_y(2)], 2: [lambda: copy_idxT(3)]})
            dve.wait_ge(k_used, 4 * NPG)
            step(V_.scalar_tensor_tensor(oX, ps[:, 4, :], dsm[:, 41:42], dcon[:, E_VE:E_VE + 512], ALU.mult, ALU.mult))
            step(V_.scalar_tensor_tensor(oY, ps[:, 5, :], dsm[:, 42:43], dcon[:, E_VE + 512:E_VE + 1024],
                                         ALU.mult, ALU.mult))
            V_.tensor_tensor(oX, oX, oY, ALU.add)
            step(V_.tensor_scalar(oL, ps[:, 6, 0:P], dsm[:, 41:42], None, ALU.mult))
            V_.scalar_tensor_tensor(oL, ps[:, 6, P:2 * P], dsm[:, 42:43], oL, ALU.mult, ALU.add).then_inc(oL_done, 1)
            dve.wait_ge(d_ps, 3)
            V_.tensor_copy(mxs[0:BD, 0:512], ps[0:BD, 3, :])
            V_.tensor_copy(mxs[0:BD, 512:1024], ps[0:BD, 2, :]).then_inc(dm_done, 1)
            rms_of(BD, ssa[0:BD, 1:3], 512)
            V_.tensor_scalar(mxs[0:BD, 0:512], mxs[0:BD, 0:512], rv[0:BD, 0:1], None, ALU.mult)
            V_.tensor_scalar(mxs[0:BD, 512:1024], mxs[0:BD, 512:1024], rv[0:BD, 1:2], None,
                             ALU.mult).then_inc(s_xn, 1)
            dve.wait_ge(s_tr, 1)
            V_.tensor_tensor(xTs, ps[:, 7, 0:64].rearrange("p (c t) -> p c t", c=DC),
                             gT[:, DC:2 * DC].unsqueeze(2).to_broadcast([P, DC, BD]), ALU.mult).then_inc(s_mT, 1)
            dve.wait_ge(s_op, 1)
            dve.wait_ge(sx_in, 16)
            for i in range(2):
                last = V_.tensor_tensor(hs[0:BD, i * 512:(i + 1) * 512], ps[0:BD, 2 + i, :],
                                        hs[0:BD, i * 512:(i + 1) * 512], ALU.add)
            last.then_inc(s_h, 1)
            rms_of(BD, ssa[0:BD, 3:4], D)
            V_.scalar_tensor_tensor(xs2, hs[0:BD, :], rv[0:BD, 0:1], gf[0:BD, :], ALU.mult, ALU.mult).then_inc(s_xn, 1)
            V_.tensor_copy(selT, ident[0:BD, 0:BD].unsqueeze(2).to_broadcast([BD, BD, P])).then_inc(selT_done, 1)
            dve.wait_ge(s_sc, 1)
            top_subkeys(SBLK, lambda hp: ps[0:BD, 2 + hp // 4, P * (hp % 4):P * (hp % 4) + P], 0, 16)
            top_experts(SBLK)
            copy_idxT(SBLK)
            V_.tensor_copy(dsm[:, 56:64], ps[:, 7, 8:16]).then_inc(s_gT, 1)
            add_y(3)
            for k in range(BD):
                q = 2 * P * NB + k
                dve.wait_ge(g[q % RING], 16 * (q // RING + 1))
                dve.wait_ge(s_xb, k + 1)
                V_.tensor_tensor_reduce(heads(ring[:, q % RING, :], P, 2), heads(ring[:, q % RING, :], P, 2),
                                        ps[:, 2 + 2 * (k % 2):4 + 2 * (k % 2), :], 1.0, 0.0, ALU.mult, ALU.add,
                                        acc[:, k:k + 1]).then_inc(s_u, 1)
            dve.wait_ge(gelu_done, NB + 1)
            w8 = W32[:, 0, 0:2, :].rearrange("p c m -> p (c m)")
            step(V_.memset(w8, 0.0))
            w8d = W32[:, 0, 0:2, :].rearrange("p c m -> p (c m)")[:, 0:64:9]
            V_.tensor_tensor(w8d, acc[:, 0:BD], dsm[:, 56:64], ALU.mult).then_inc(W_done, 1)
            dve.wait_ge(s_v, 1)
            for i in range(2):
                last = V_.tensor_tensor(hs[0:BD, i * 512:(i + 1) * 512], ps[0:BD, i, :],
                                        hs[0:BD, i * 512:(i + 1) * 512], ALU.add)
            last.then_inc(y_done, 1)

        @block.tensor
        def _(pe):
            T_ = nc.tensor
            pe.wait_ge(const_in, 16 * 7)

            def transposes(src, banks, n):
                for c in range(DC):
                    last = T_.transpose(ps[:, banks[c // 4], (c % 4) * n:(c % 4) * n + n],
                                        src[0:n, c * P:(c + 1) * P], ident[0:n, 0:n])
                last.then_inc(tr_ps, 1)

            for b in range(NB + 1):
                n = ROWS[b]
                pe.wait_ge(xn_done, b + 1 + min(b, NB))
                transposes(mx, (5, 6), n)
                pe.wait_ge(xnT_done, b + 1)
                for i in range(5):
                    w = 512 if i < 4 else TAIL
                    for c in range(DC):
                        if b == 0 and i == 0:
                            pe.wait_ge(win_in, 16 * DC)
                        last = T_.matmul(ps[0:n, i, 0:w], xnT[:, c, 0:n], win[:, c, 512 * i:512 * i + w],
                                         start=(c == 0), stop=(c == DC - 1))
                    last.then_inc(proj_ps, 1)
                pe.wait_ge(ckv_done, b + 1)
                T_.transpose(ps[:, 7, 0:n], ckvn[0:n, :], ident[0:n, 0:n]).then_inc(ckv_ps, 1)
                pe.wait_ge(ckvT_done, b + 1)
                T_.matmul(ps[0:n, 5, :], ckvT[:, 0:n], wk, start=True, stop=True)
                T_.matmul(ps[0:n, 6, :], ckvT[:, 0:n], wv, start=True, stop=True).then_inc(kv_ps, 1)
                if b == SBLK:
                    break
                pe.wait_ge(lf_done, b + 1)
                for a in range(b + 1):
                    lhs = con[:, C_TRI:C_TRI + P] if a == b else con[:, C_ONES:C_ONES + P]
                    last = T_.matmul(ps[:, 7, 256:256 + H], lhs, lf[:, a, :], start=(a == 0), stop=(a == b))
                last.then_inc(c_ps, 1)
                pe.wait_ge(qk_done, b + 1)
                pe.wait_ge(v_done, 2 * (b + 1))
                for gi in range(8):
                    kd, fox = (KM, 0) if gi % 4 < 2 else (KF, 1)
                    src = Qk if gi < 4 else Kk
                    for j in range(4):
                        h = 4 * (gi % 2) + j
                        o = (H * KM if fox else 0) + h * kd
                        last = T_.transpose(ps[0:kd, QKB[gi], j * P:(j + 1) * P], src[:, o:o + kd], ident)
                    last.then_inc(qk_ps, 1)
                pe.wait_ge(qk_even, 4 * (b + 1))
                pe.wait_ge(qk_odd, 4 * (b + 1))
                w = (b + 1) * P

                def scores(hh):
                    kd = KM if hh < 8 else KF
                    if hh >= 2:
                        pe.wait_ge(exp_done, 16 * b + hh - 1)
                    T_.matmul(ps[:, 2 + hh % 2, 0:w], QT[0:kd, hh, :], KT[0:kd, hh, 0:w],
                              start=True, stop=True).then_inc(s_ps, 1)

                def turn(hh):
                    pe.wait_ge(exp_done, 16 * b + hh + 1)
                    if hh >= 2:
                        pe.wait_ge(pT_done[hh % 2], 8 * b + hh // 2)
                    for a in range(b + 1):
                        last = T_.transpose(ps[:, 4 + hh % 2, a * P:(a + 1) * P], Pm[:, hh % 2, a * P:(a + 1) * P],
                                            ident)
                    last.then_inc(pT_ps, 1)

                def values(hh):
                    pe.wait_ge(pT_done[hh % 2], 8 * b + hh // 2 + 1)
                    for a in range(b + 1):
                        last = T_.matmul(ps[:, hh // 8, VD * (hh % 8):VD * (hh % 8) + VD],
                                         PT[:, hh % 2, a * P:(a + 1) * P], V[:, a, VD * hh:VD * hh + VD],
                                         start=(a == 0), stop=(a == b))
                    last.then_inc(o_ps, 1)

                scores(0)
                for hh in range(16):
                    if hh + 1 < 16:
                        scores(hh + 1)
                    turn(hh)
                    if hh:
                        values(hh - 1)
                values(15)
                pe.wait_ge(xn_done, 2 * (b + 1))
                transposes(mx, (6, 7), P)

            pe.wait_ge(wo_in, 16 * DC)

            def project(b):
                if b:
                    pe.wait_ge(sc_done, b)
                for i in range(2):
                    for c in range(DC):
                        last = T_.matmul(ps[:, i, :], mixT[:, b, c, :], wo[:, c, 512 * i:512 * i + 512],
                                         start=(c == 0), stop=(c == DC - 1))
                last.then_inc(op_ps, 1)

            def route(b):
                pe.wait_ge(xn2_done, b + 1)
                transposes(xn2[:, b, :], (6, 7), P)
                pe.wait_ge(xnT2_done, b + 1)
                if b == 0:
                    pe.wait_ge(wq_in, 16 * DC)
                    pe.wait_ge(sk_in, 16)
                for hp in range(NHP):
                    for c in range(DC):
                        last = T_.matmul(ps[:, 2 + hp // 4, P * (hp % 4):P * (hp % 4) + P],
                                         wq[:, c, P * hp:P * hp + P], hb[:, c * P:(c + 1) * P],
                                         start=(c == 0), stop=(c == DC - 1))
                last.then_inc(q_ps, 1)
                pe.wait_ge(q_done, b + 1)
                for hp in range(NHP):
                    last = T_.matmul(ps[:, (6, 7, 0, 1)[hp // 4], P * (hp % 4):P * (hp % 4) + P], qpT[:, hp, :],
                                     skT[:, hp, :], start=True, stop=True)
                last.then_inc(sc_ps, 1)

            for b in range(NB):
                project(b)
                route(b)

            def turn_idx(b):
                n = ROWS[b]
                pe.wait_ge(top_done, b + 1)
                pe.wait_ge(sc_done, NB)
                if b:
                    pe.wait_ge(W_done, b)
                T_.transpose(ps[:, 7, 0:n], eidf[0:n, :], ident[0:n, 0:n]).then_inc(idx_ps, 1)

            def turn_w(b):
                pe.wait_ge(w_done, b + 1)
                pe.wait_ge(idxT_done, b + 1)
                T_.transpose(ps[:, 7, 0:P], acc[:, :], ident).then_inc(w_ps, 1)

            def v_phase(b):
                pe.wait_ge(W_done, b + 1)
                if b:
                    pe.wait_ge(y_done, b)
                for k in range(P):
                    q = 2 * P * b + P + k
                    c, j = k // 4, k % 4
                    pe.wait_ge(g[q % RING], 16 * (q // RING + 1))
                    for i in range(2):
                        last = T_.matmul(ps[32 * j:32 * j + 32, i, :], W32[:, j, c, :],
                                         ring[:, q % RING, 512 * i:512 * i + 512], start=(c == 0), stop=(c == 31),
                                         tile_position=(0, 32 * j), skip_group_check=True)
                    last.then_inc(v_used, 1)

            turn_idx(0)
            pe.wait_ge(dq_in, 1)
            for c in range(8):
                T_.transpose(ps[:, 6, 8 * c:8 * c + 8], SR[0:BD, 2048 + P * c:2048 + P * (c + 1)], ident[0:BD, 0:BD])
            for h in range(H):
                last = T_.transpose(ps[0:RP, 6, 64 + 8 * h:72 + 8 * h], SB[0:BD, KM * h + NOPE:KM * (h + 1)],
                                    ident[0:BD, 0:BD])
            last.then_inc(d_ps, 1)
            pe.wait_ge(dq_in, 2)
            for i in range(2):
                T_.matmul(ps[:, 6, 128 + i:129 + i], dsm[0:BD, 64 + 128 * i:192 + 128 * i],
                          con[0:BD, C_ONES:C_ONES + 1], start=True, stop=True)
            for q in range(4):
                last = T_.matmul(ps[:, 6, 256 + 16 * q:272 + 16 * q], wkTd[:, q, :], qbd[:, q, :],
                                 start=True, stop=True)
            last.then_inc(d_ps, 1)
            pe.sem_inc(sqd_used, 2)
            turn_w(0)
            v_phase(0)
            turn_idx(1)
            pe.wait_ge(dq_done, 2)

            def decode_scores(first, last_it):
                with pe.Fori(first, last_it) as it:
                    for s in range(2):

                        def key_norm(par, q):
                            m = (2 * s + par) * 4 + q
                            pe.wait_ge(sqd_done, pe.snap(it * 16 + (m + 1)))
                            T_.matmul(ps[:, 2 + q % 2, :], wkd[:, q * P:(q + 1) * P], kbuf[:, par, :, 512:640],
                                      start=True, stop=True).then_inc(n_ps, 1)

                        def norm_sum(par, q, final=None):
                            m = (2 * s + par) * 4 + q
                            pe.wait_ge(sqd_done, pe.snap(it * 16 + (m + 3)))
                            for j in range(4):
                                last = T_.matmul(ps[32 * j:32 * j + 32, 4 + s, 2 * P:3 * P],
                                                 dcon[:, E_HM + 32 * (4 * par + q):E_HM + 32 * (4 * par + q) + 32],
                                                 sqd[:, q % 2, j * P:(j + 1) * P],
                                                 start=False, stop=(par == 1 and q == 3),
                                                 tile_position=(0, 32 * j), skip_group_check=True)
                            last.then_inc(sqd_used, 1)

                        pe.wait_ge(abr_done, pe.snap(it * 2 + (s + 1)))
                        pe.sem_inc(p_step, 1)
                        for par in range(2):
                            pe.wait_ge(k_in[par], pe.snap(it * 256 + (128 * s + 128)))
                            pe.sem_inc(p_step, 1)
                            key_norm(par, 0)
                            key_norm(par, 1)
                            for c in range(4):
                                for j in range(4):
                                    T_.matmul(ps[32 * j:32 * j + 32, 4 + s, 0:P], qz[:, c, 2 * j + par, :],
                                              kbuf[:, par, j, c * P:(c + 1) * P], start=(par == 0 and c == 0),
                                              stop=False, tile_position=(0, 32 * j), skip_group_check=True)
                            norm_sum(par, 0)
                            key_norm(par, 2)
                            for j in range(4):
                                T_.matmul(ps[32 * j:32 * j + 32, 4 + s, P:2 * P], qz[:, 4, 2 * j + par, :],
                                          kbuf[:, par, j, 512:640], start=False, stop=(par == 1),
                                          tile_position=(0, 32 * j), skip_group_check=True)
                            norm_sum(par, 1)
                            key_norm(par, 3)
                            for j in range(4):
                                last = T_.matmul(ps[32 * j:32 * j + 32, 4 + s, 0:P], qpz[0:RP, 2 * j + par, :],
                                                 kpb[0:RP, par, j, :], start=False, stop=(par == 1),
                                                 tile_position=(0, 32 * j), skip_group_check=True)
                            last.then_inc(k_used, 1)
                            norm_sum(par, 2)
                            norm_sum(par, 3)

            decode_scores(0, 8)
            turn_w(1)
            v_phase(1)
            turn_idx(2)
            decode_scores(8, 16)
            turn_w(2)
            v_phase(2)
            turn_idx(3)
            pe.sem_inc(pd_ps, 2)
            pe.wait_ge(dq_done, 3)
            T_.transpose(ps[0:BD, 2, 256:384], dsm[:, 48:56], ident).then_inc(pd_ps, 1)
            pe.wait_ge(dq_done, 4)
            pe.wait_ge(v_in, 48)
            for k in range(2):
                T_.matmul(ps[:, 4 + k, :], pself, sqd[0:BD, 0, :], start=True, stop=False, skip_group_check=True)
            T_.matmul(ps[:, 6, 0:2 * P], pself, sqd[0:BD, 1, 0:R].unsqueeze(1).to_broadcast([BD, 2, R]),
                      start=True, stop=False, skip_group_check=True)
            with pe.Fori(0, NPG // 2) as it:
                for s in range(2):
                    pe.wait_ge(stg_done, pe.snap(it * 2 + (s + 1)))
                    pe.sem_inc(p_step, 1)
                    pe.wait_ge(pd_done, pe.snap(it * 2 + (s + 1)))
                    T_.transpose(ps[:, 2 + s, 0:P], stg[:, s, :], ident).then_inc(pd_ps, 1)
                    pe.wait_ge(pd_done, pe.snap(it * 2 + (s + 3)))
                    pe.sem_inc(p_step, 1)
                    for par in range(2):
                        pe.wait_ge(k_in[par], pe.snap(it * 128 + (128 * NPG + 64 * s + 64)))
                        pe.sem_inc(p_step, 1)
                        for j in range(4):
                            T_.matmul(ps[32 * j:32 * j + 32, 4 + par, :], pTd[:, s, 32 * j:32 * j + 32],
                                      kbuf[:, par, j, 0:512], start=False, stop=True,
                                      tile_position=(0, 32 * j), skip_group_check=True)
                        for j in range(4):
                            last = T_.matmul(ps[32 * j:32 * j + 32, 6, par * P:(par + 1) * P],
                                             pTd[:, s, 32 * j:32 * j + 32], kbuf[:, par, j, 512:640],
                                             start=False, stop=True, tile_position=(0, 32 * j),
                                             skip_group_check=True)
                        last.then_inc(k_used, 1)
            turn_w(3)
            v_phase(3)
            pe.wait_ge(oL_done, 1)
            T_.transpose(ps[:, 7, 0:P], oL, ident).then_inc(oLT_ps, 1)
            pe.wait_ge(s_sum, 1)
            T_.matmul(ps[0:BD, 2, :], dcon[:, E_B:E_B + BD], oX, start=True, stop=True)
            for h in range(H):
                last = T_.matmul(ps[0:BD, 3, VD * h:VD * h + VD], oLT[:, 8 + h::16], wvs[:, VD * h:VD * h + VD],
                                 start=True, stop=True)
            last.then_inc(d_ps, 1)
            pe.wait_ge(s_xn, 1)
            for c in range(DC):
                last = T_.transpose(ps[:, 7, 8 * c:8 * c + 8], mxs[0:BD, c * P:(c + 1) * P], ident[0:BD, 0:BD])
            last.then_inc(s_tr, 1)
            pe.wait_ge(s_mT, 1)
            pe.wait_ge(swo_in, 16 * DC)
            for i in range(2):
                for c in range(DC):
                    last = T_.matmul(ps[0:BD, 2 + i, :], xTs[:, c, :], wo_s[:, c, 512 * i:512 * i + 512],
                                     start=(c == 0), stop=(c == DC - 1))
            last.then_inc(s_op, 1)
            pe.wait_ge(s_xn, 2)
            for c in range(DC):
                last = T_.transpose(ps[:, 7, 8 * c:8 * c + 8], xs2[:, c * P:(c + 1) * P], ident[0:BD, 0:BD])
            last.then_inc(s_tr, 1)
            pe.wait_ge(s_xT, 1)
            pe.wait_ge(swq_in, 16 * DC)
            for hp in range(NHP):
                for c in range(DC):
                    last = T_.matmul(ps[:, 6, 8 * hp:8 * hp + 8], wq_s[c][:, P * hp:P * hp + P], xTs[:, c, :],
                                     start=(c == 0), stop=(c == DC - 1))
            last.then_inc(s_q, 1)
            pe.wait_ge(s_qT, 1)
            pe.wait_ge(ssk_in, 16)
            for hp in range(NHP):
                last = T_.matmul(ps[0:BD, 2 + hp // 4, P * (hp % 4):P * (hp % 4) + P], qTs[:, hp, :],
                                 skT_s[:, hp, :], start=True, stop=True)
            last.then_inc(s_sc, 1)
            pe.wait_ge(gates_done, NB + 1)
            T_.transpose(ps[:, 7, 8:16], gate[0:BD, 0, :], ident[0:BD, 0:BD])
            turn_idx(SBLK)
            pe.wait_ge(selT_done, 1)
            pe.wait_ge(s_gT, 1)
            for k in range(BD):
                if k >= 2:
                    pe.wait_ge(s_u, k - 1)
                for i in range(2):
                    last = T_.matmul(ps[:, 2 + 2 * (k % 2) + i, :], selT[:, k, :], xs2[:, 512 * i:512 * i + 512],
                                     start=True, stop=True)
                last.then_inc(s_xb, 1)
            pe.wait_ge(W_done, NB + 1)
            pe.wait_ge(y_done, NB)
            w8 = W32[:, 0, 0:2, :].rearrange("p c m -> p (c m)")
            for k in range(BD):
                q = 2 * P * NB + BD + k
                pe.wait_ge(g[q % RING], 16 * (q // RING + 1))
                for i in range(2):
                    last = T_.matmul(ps[0:BD, i, :], w8[:, 8 * k:8 * k + 8],
                                     ring[:, q % RING, 512 * i:512 * i + 512], start=(k == 0), stop=(k == BD - 1))
            last.then_inc(s_v, 1)


_OUTS = [
    ((1, T, D)), ((BD, 1, D)), ((1, 1, T, R)), ((1, 1, T, RP)), ((1, 1, T, H, FD)), ((1, 1, T, H, FD)), ((1, 1, T, H)),
    ((1, BD, 1, R)), ((1, BD, 1, RP)), ((1, BD, 1, H, FD)), ((1, BD, 1, H, FD)), ((1, BD, 1, H)),
]
_FLAT = [(T, D), (BD, D), (T, R), (T, RP), (T, H * FD), (T, H * FD), (T, H),
         (BD, R), (BD, RP), (BD, H * FD), (BD, H * FD), (BD, H)]
_NAMES = ["y_prompt", "y_sample", "lat_p", "kpe_p", "fk_p", "fv_p", "lf_p", "lat_s", "kpe_s", "fk_s", "fv_s", "lf_s"]


def _constants():
    c = np.zeros((P, C_END), np.float32)
    i, j = np.arange(P)[:, None], np.arange(P)[None, :]
    c[:, C_ID:C_ID + P] = i == j
    c[:, C_MASK:C_MASK + P] = np.where(j <= i, 0.0, NEG)
    c[:, C_TRI:C_TRI + P] = i <= j
    c[:, C_ONES:C_ONES + P] = 1.0
    half = RP // 2
    inv = np.power(np.float32(10000.0), -np.arange(half, dtype=np.float32) / np.float32(half)).astype(np.float32)
    pos = np.stack([np.arange(P) + b * P for b in range(NB)] + [np.full(P, PAST)], 1).astype(np.float32)
    ang = pos[:, :, None] * inv
    c[:, C_COS:C_SIN] = np.cos(ang).reshape(P, -1)
    c[:, C_SIN:C_DIM] = np.sin(ang).reshape(P, -1)
    c[:, C_DIM:C_IOTA] = [1.0 / NOPE] * 24 + [1.0 / RP] * 8 + [1.0 / R, 1.0 / RP]
    c[:, C_IOTA:C_END] = np.arange(16)
    return c


def _decode_constants():
    e = np.zeros((P, E_END), np.float32)
    for par in range(2):
        for q in range(4):
            for half in range(2):
                e[64 * half:64 * half + 64, E_HM + 32 * (4 * par + q) + 16 * par + 8 + 2 * q + half] = 1.0
    for row in range(P):
        b, h = row // 16, row % 16
        e[b, E_BT + row] = 1.0
        e[row, E_B + b] = 1.0
        if h < H:
            a = E_VE + 512 * (b % 2) + FD * h
            e[row, a:a + FD] = 1.0
        e[row, E_PAR + b % 2] = 1.0
        e[row, E_MOD] = h
    return e


def _layout(x_prompt, x_sample, cache_mla_latent, cache_mla_kpe, cache_fox_k, cache_fox_v, cache_fox_logf,
            page_table, g_attn, w_in, b_forget, g_q_nope, g_q_pe, g_ckv, g_k_pe, w_ukv, g_k_nope,
            g_fox_q, g_fox_k, g_out_mla, g_out_fox, w_o, g_ffn, w_peer_q, peer_sub_keys, peer_u, peer_v):
    n = cache_mla_latent.shape[1]
    cols = np.split(w_in[0], np.cumsum([512, 256, 128, 32, 512, 512, 512]), axis=1)
    win = np.concatenate([cols[0], cols[4], cols[5], cols[6], cols[1], cols[2], cols[3], cols[7]], axis=1)
    ukv = w_ukv[0].reshape(R, H, NOPE + VD)
    w_k = np.ascontiguousarray(ukv[:, :, :NOPE]).reshape(R, H * NOPE)
    w_v = np.ascontiguousarray(ukv[:, :, NOPE:]).reshape(R, H * VD)
    chunks = lambda w: w.reshape(DC, P, -1).transpose(1, 0, 2)
    lat, fox_k = cache_mla_latent[0], cache_fox_k[0].reshape(n, PAGE, 4, P)
    fox_v = cache_fox_v[0].reshape(n, PAGE, H * FD)
    logf = np.zeros((n, 16, PAGE), np.float32)
    logf[:, :H] = cache_fox_logf[0].transpose(0, 2, 1)
    pages = page_table.reshape(4, 2, NPG).transpose(2, 1, 0).reshape(1, -1)
    return {
        "x_prompt": x_prompt.reshape(T, D), "x_sample": x_sample.reshape(BD, D),
        "w_in": chunks(win), "w_k": w_k, "w_v": w_v,
        "w_kT": w_k.T.reshape(4, P, R).transpose(1, 0, 2),
        "w_o": chunks(w_o[0]), "w_q": chunks(w_peer_q[0]),
        "sub_keys": peer_sub_keys[0].reshape(NHP, P, P).transpose(2, 0, 1),
        "gains": np.concatenate([g_q_nope[0], g_q_pe[0], g_ckv[0], g_k_pe[0], g_k_nope[0], g_fox_q[0], g_fox_k[0],
                                 b_forget[0]]),
        "g_cols": np.concatenate([g_attn[0].reshape(DC, P), g_out_mla[0].reshape(4, P), g_out_fox[0].reshape(4, P)]).T,
        "g_ffn": g_ffn[0], "consts": _constants(), "dec_consts": _decode_constants(),
        "pages": pages, "page_rows": np.repeat(page_table, 16, axis=0),
        "kt_pool": np.concatenate([fox_k.transpose(0, 3, 2, 1).reshape(n, P, 4 * PAGE), lat.transpose(0, 2, 1)], axis=2),
        "kpe_pool": cache_mla_kpe[0].transpose(0, 2, 1),
        "vn_pool": np.concatenate([fox_v, lat], axis=2),
        "logf_pool": logf.reshape(n * 16, PAGE),
        "peer_u": peer_u[0], "peer_v": peer_v[0],
    }


def kernel(**inputs):
    import concourse.bacc as bacc
    from concourse.bass_utils import run_bass_kernel_spmd

    arrays = {k: np.ascontiguousarray(v) for k, v in _layout(**{k: np.asarray(v) for k, v in inputs.items()}).items()}
    nc = bacc.Bacc("TRN2", target_bir_lowering=False, num_devices=1)
    args = {k: nc.dram_tensor(k, a.shape, mybir.dt.from_np(a.dtype), kind="ExternalInput").ap()
            for k, a in arrays.items()}
    for name, shape in zip(_NAMES, _FLAT):
        args[name] = nc.dram_tensor(name, shape, F32, kind="ExternalOutput").ap()
    build(nc, **args)
    got = run_bass_kernel_spmd(nc, [arrays], core_ids=[0]).results[0]
    return tuple(got[name].reshape(shape) for name, shape in zip(_NAMES, _OUTS))
```

```python
from contextlib import ExitStack

import numpy as np

import concourse.bass as bass
from concourse import mybir

ALU = mybir.AluOpType
ACT = mybir.ActivationFunctionType
AX = mybir.AxisListType
F32 = mybir.dt.float32
U32 = mybir.dt.uint32
I32 = mybir.dt.int32

P = 128
D = 1024
DC = D // P
T = 512
NB = T // P
BD = 8
PAST = 4096
PAGE = 128
NPG = PAST // PAGE
H = 8
NOPE = 64
RP = 32
VD = 64
R = 128
FD = 64
KM = NOPE + RP
KF = FD + 2
QW = H * (KM + KF)
WIN = 2472
PHEADS = 8
NHP = 2 * PHEADS
TOPK = 16
SLOTS = PHEADS * TOPK
EPS = 1e-6
S_MLA = float(KM) ** -0.5
S_FOX = float(FD) ** -0.5
NEG = -1e30
RING = 8
U_LAST = [128, 128, 128, 116]
U_AHEAD = [8, 3, 3, 2]
TAIL_QPE, TAIL_CKV, TAIL_KPE, TAIL_F = 0, 256, 384, 416
TAIL = 424
G_QN, G_QPE, G_CKV, G_KPE, G_KN, G_FQ, G_FK, G_BF = 0, 64, 96, 224, 256, 320, 384, 448
GS = 456
C_ID, C_MASK, C_TRI, C_ONES, C_COS, C_SIN, C_DIM, C_IOTA, C_END = 0, 128, 256, 384, 512, 592, 672, 706, 722
E_HM, E_BT, E_B, E_VE, E_PAR, E_MOD, E_END = 0, 256, 384, 392, 1416, 1418, 1420


def build(nc, x_prompt, x_sample, w_in, w_k, w_v, w_kT, w_o, w_q, sub_keys, gains, g_cols, g_ffn, consts, dec_consts,
          pages, page_rows, kt_pool, kpe_pool, vn_pool, logf_pool, peer_u, peer_v,
          y_prompt, y_sample, lat_p, kpe_p, fk_p, fv_p, lf_p, lat_s, kpe_s, fk_s, fv_s, lf_s):
    ctx = ExitStack()
    with ctx:
        def sb(name, shape, dt=F32):
            return ctx.enter_context(nc.sbuf_tensor(name, shape, dt))

        def sem(name):
            return ctx.enter_context(nc.semaphore(name))

        h_dram = nc.dram_tensor("h_scratch", (NB * P + BD, D), F32, kind="Internal").ap()
        qs_dram = nc.dram_tensor("q_scratch", (BD, QW), F32, kind="Internal").ap()
        ks_dram = nc.dram_tensor("k_scratch", (BD, QW), F32, kind="Internal").ap()
        vs_dram = nc.dram_tensor("v_scratch", (BD, H * FD), F32, kind="Internal").ap()
        cs_dram = nc.dram_tensor("c_scratch", (BD, R), F32, kind="Internal").ap()

        KB = 256
        arena = sb("arena", [P, 184 * KB])

        def part(kib, n):
            a = int(kib * KB)
            return arena[:, a:a + n]

        win = part(0, DC * WIN).rearrange("p (c n) -> p c n", c=DC)
        KT = part(77.5, 16 * T).rearrange("p (h t) -> p h t", h=16)
        V = part(109.5, NB * D).rearrange("p (b n) -> p b n", b=NB)
        QT = part(125.5, 16 * P).rearrange("p (h t) -> p h t", h=16)
        Qk = part(133.5, QW)
        Kk = part(133.5 + 5.0625, QW)
        mixT = part(144, NB * D).rearrange("p (b c t) -> p b c t", b=NB, c=DC)
        xn2 = part(144, NB * D).rearrange("p (b n) -> p b n", b=NB)
        sq = part(160, 2048)
        Pm = part(160, 1024).rearrange("p (i n) -> p i n", i=2)
        PT = part(164, 1024).rearrange("p (i n) -> p i n", i=2)
        mx = part(168, D)
        xnT_flat = part(172, D)
        xnT = part(172, D).rearrange("p (c t) -> p c t", c=DC)
        wk = part(176, 512)
        wv = part(178, 512)
        pe9 = part(180, 288).rearrange("p (h d) -> p h d", h=9)
        rp9 = part(181.25, 288).rearrange("p (h d) -> p h d", h=9)
        rt = part(182.5, 288).rearrange("p (i h d) -> p i h d", i=2, h=9)
        wq = part(0, DC * 2048).rearrange("p (c n) -> p c n", c=DC)
        wo = part(64, DC * D).rearrange("p (c n) -> p c n", c=DC)
        qpT = part(128, NHP * P).rearrange("p (g t) -> p g t", g=NHP)
        skT = part(136, NHP * P).rearrange("p (g k) -> p g k", g=NHP)
        sc = part(160, 3 * NHP * P).rearrange("p (i g k) -> p i g k", i=3, g=NHP)
        ring = part(96, RING * D).rearrange("p (s n) -> p s n", s=RING)
        W32 = part(128, 4 * 32 * 32).rearrange("p (j c m) -> p j c m", j=4, c=32)
        SA = part(0, PAST)
        SB = part(16, PAST)
        SR = part(32, PAST)
        SABR = part(0, 3 * PAST).rearrange("p (k n) -> p k n", k=3)
        kbuf = part(48, 2 * 4 * 640).rearrange("p (i j n) -> p i j n", i=2, j=4)
        kpb = part(68, 2 * 4 * 128).rearrange("p (i j n) -> p i j n", i=2, j=4)
        sqd = part(72, 1024).rearrange("p (i n) -> p i n", i=2)
        pTd = part(76, 256).rearrange("p (i n) -> p i n", i=2)
        dcon = part(77, E_END)
        wkd = part(83, 512)
        wkTd = part(85, 512).rearrange("p (q r) -> p q r", q=4)
        qz = part(87, 5 * BD * 32).rearrange("p (c b m) -> p c b m", c=5, b=BD)
        qpz = part(92, BD * 32).rearrange("p (b m) -> p b m", b=BD)
        qTd = part(93, 8 * BD).rearrange("p (c b) -> p c b", c=8)
        qbd = part(93.25, 4 * 16).rearrange("p (q m) -> p q m", q=4)
        qpT8 = part(93.5, 8 * BD).rearrange("p (h b) -> p h b", h=8)
        dsm = part(94, 512)
        stg = part(93, 256).rearrange("p (i n) -> p i n", i=2)
        wo_s = part(16, DC * D).rearrange("p (c n) -> p c n", c=DC)
        WQ_S = [160, 168, 176, 0, 8, 48, 56, 144]
        wq_s = [part(k, 2048) for k in WQ_S]
        skT_s = part(152, 2048).rearrange("p (g k) -> p g k", g=NHP)
        oX = part(83, 512)
        qrow = oX
        oL = part(85, 128)
        oLT = part(85.5, 128)
        mxs = part(87, D)
        xTs = part(91, 64).rearrange("p (c t) -> p c t", c=DC)
        qTs = part(91.25, 128).rearrange("p (g t) -> p g t", g=NHP)
        wvs = part(68, 512)
        xs2 = part(64, D)[0:BD, :]
        selT = part(68, D)[0:BD, :].rearrange("p (t m) -> p t m", t=BD)
        oY = part(89, 512)
        pself = part(86, P)[0:BD, :]
        kscr = part(48, PAST)
        LG = part(168, PAST)
        lgf = dsm[:, 320:352]
        lgi = dsm[:, 352:384].bitcast(U32)
        prow = dsm[:, 384:416].bitcast(I32)
        Wd = W32[:, :, :, :].rearrange("p j c m -> p j (c m)")[:, :, 0:1024:33]
        SCB = [6, 7, 0, 1]
        QKB = [7, 0, 1, 2, 3, 4, 5, 6]
        hs = part(72, D)
        hb = sb("hb", [P, D])
        gf = sb("gf", [P, D])
        con = sb("con", [P, C_END])
        gs = sb("gs", [P, GS])
        gT = sb("gT", [P, 2 * DC])
        ssa = sb("ssa", [P, 4])
        ssv = sb("ssv", [P, 34])
        lnv = sb("lnv", [P, 34])
        r0v = sb("r0v", [P, 34])
        rv = sb("rv", [P, 34])
        tv = sb("tv", [P, 34])
        ckvn = sb("ckvn", [P, R])
        eidf = ckvn
        lf = sb("lf", [P, 5, H])
        fz = sb("fz", [P, 4, H])
        nmx = sb("nmx", [P, 16])
        rs = sb("rs", [P, 16])
        eidx = sb("eidx", [P, SLOTS], U32)
        idxT = sb("idxT", [P, P], U32)
        gate = sb("gate", [P, 2, SLOTS])
        acc = sb("acc", [P, SLOTS])
        ckvT = acc
        topv = sb("topv", [P, NHP, TOPK])
        topi = sb("topi", [P, NHP, TOPK], U32)
        topf = sb("topf", [P, NHP, TOPK])
        mrep = sb("mrep", [P, 256])
        ptab = sb("ptab", [1, BD * NPG], I32)
        idxS = sb("idxS", [P, BD], U32)

        ps = ctx.enter_context(nc.psum_tensor("ps", [P, 8, 512], F32))
        ident = con[:, C_ID:C_ID + P]

        const_in = sem("const_in")
        const2_in = sem("const2_in")
        win_in = [sem(f"win_in{c}") for c in range(DC)]
        wq_in = sem("wq_in")
        wo_in = sem("wo_in")
        sk_in = sem("sk_in")
        x_in = sem("x_in")
        h_in = sem("h_in")
        h_made = sem("h_made")
        h_stored = sem("h_stored")
        stored = sem("stored")
        rows_out = sem("rows_out")
        s_rows = sem("s_rows")
        sumsq = sem("sumsq")
        rms_in = sem("rms_in")
        rms_out = sem("rms_out")
        x_norm = sem("x_norm")
        m_norm = sem("m_norm")
        x_tr = sem("x_tr")
        m_tr = sem("m_tr")
        tr_ps = sem("tr_ps")
        xnT_done = sem("xnT_done")
        proj_ps = sem("proj_ps")
        sq_done = sem("sq_done")
        ckv_done = sem("ckv_done")
        ckv_ps = sem("ckv_ps")
        ckvT_done = sem("ckvT_done")
        kv_ps = sem("kv_ps")
        v_done = sem("v_done")
        xnT2_done = sem("xnT2_done")
        fz_done = sem("fz_done")
        fexp_done = sem("fexp_done")
        lf_done = sem("lf_done")
        c_ps = sem("c_ps")
        rp_done = sem("rp_done")
        rp_copied = sem("rp_copied")
        qk_done = sem("qk_done")
        qk_ps = sem("qk_ps")
        qk_even = sem("qk_even")
        qk_odd = sem("qk_odd")
        s_ps = sem("s_ps")
        max_done = sem("max_done")
        exp_done = sem("exp_done")
        pT_ps = sem("pT_ps")
        pT_done = [sem("pT_done_even"), sem("pT_done_odd")]
        o_ps = sem("o_ps")
        mx_done = sem("mx_done")
        mixT_done = sem("mixT_done")
        op_ps = sem("op_ps")
        xn2_done = sem("xn2_done")
        q_ps = sem("q_ps")
        q_done = sem("q_done")
        sc_ps = sem("sc_ps")
        sc_done = sem("sc_done")
        gexp_in = sem("gexp_in")
        gexp_out = sem("gexp_out")
        top_done = sem("top_done")
        idx_ps = sem("idx_ps")
        idxT_done = sem("idxT_done")
        g = [sem(f"gathered{i}") for i in range(RING)]
        u_used = sem("u_used")
        v_used = sem("v_used")
        gelu_done = sem("gelu_done")
        w_done = sem("w_done")
        w_ps = sem("w_ps")
        W_done = sem("W_done")
        y_done = sem("y_done")
        scalar_waited = sem("scalar_waited")
        dm_done = sem("dm_done")
        s_mT = sem("s_mT")
        s_h = sem("s_h")
        s_gT = sem("s_gT")
        ssk_in = sem("ssk_in")
        gates_done = sem("gates_done")
        oL_done = sem("oL_done")
        oLT_ps = sem("oLT_ps")
        v_step = sem("v_step")
        a_step = sem("a_step")
        tensor_waited = sem("tensor_waited")
        sync_waited = sem("sync_waited")
        dec_in = sem("dec_in")
        k_in = [sem("k_in0"), sem("k_in1")]
        k_used = sem("k_used")
        n_ps = sem("n_ps")
        sqd_done = sem("sqd_done")
        sqd_used = sem("sqd_used")
        abr_done = sem("abr_done")
        dq_done = sem("dq_done")
        d_ps = sem("d_ps")
        stg_done = sem("stg_done")
        lg_gathered = sem("lg_gathered")
        dq_in = sem("dq_in")
        s_sum = sem("s_sum")
        s_op = sem("s_op")
        s_xn = sem("s_xn")
        s_tr = sem("s_tr")
        s_xT = sem("s_xT")
        s_q = sem("s_q")
        s_qr = sem("s_qr")
        s_qt = sem("s_qt")
        s_qT = sem("s_qT")
        s_sc = sem("s_sc")
        s_u = sem("s_u")
        s_xb = sem("s_xb")
        s_v = sem("s_v")
        selT_done = sem("selT_done")
        v_in = sem("v_in")
        sx_in = sem("sx_in")
        swo_in = sem("swo_in")
        swq_in = sem("swq_in")
        d_sb = sem("d_sb")
        soft_in = sem("soft_in")
        soft_ln = sem("soft_ln")
        soft_max = sem("soft_max")
        soft_exp = sem("soft_exp")
        lg_in = sem("lg_in")
        pd_ps = sem("pd_ps")
        pd_done = sem("pd_done")

        block = ctx.enter_context(nc.Block())

        ROWS = [P] * NB + [BD]
        SBLK = NB
        PROJ_ORDER = [3, 2, 4, 0, 1]
        ORDER = [SBLK] + list(range(NB))
        def gcol(i):
            return 32 * (i % 4) + i // 4

        @block.sync
        def _(sp):
            sp.dma_start(con[:, :], consts).then_inc(const_in, 16)
            sp.dma_start(gs[:, :], gains.partition_broadcast(P)).then_inc(const_in, 16)
            sp.dma_start(gT[:, :], g_cols).then_inc(const_in, 16)
            sp.dma_start(hb[0:BD, :], x_sample).then_inc(x_in, 16)
            for c in range(DC):
                sp.dma_start(win[:, c, :], w_in[:, c, :]).then_inc(win_in[c], 16)
            sp.dma_start(wk, w_k).then_inc(const2_in, 16)
            sp.dma_start(wv, w_v).then_inc(const2_in, 16)
            sp.dma_start(gf[:, :], g_ffn.partition_broadcast(P)).then_inc(const2_in, 16)
            sp.dma_start(ptab[:, :], pages).then_inc(const2_in, 16)
            for t, b in enumerate(ORDER):
                n = ROWS[b]
                if t < NB:
                    sp.wait_ge(x_tr, t + 1)
                    sp.dma_start(hb[:, :], x_prompt[t * P:(t + 1) * P, :]).then_inc(x_in, 16)
                outs = ([lat_p[b * P:(b + 1) * P], kpe_p[b * P:(b + 1) * P], fk_p[b * P:(b + 1) * P],
                         fv_p[b * P:(b + 1) * P], lf_p[b * P:(b + 1) * P]] if b < NB
                        else [lat_s, kpe_s, fk_s, fv_s, lf_s])
                vb = b if b < NB else 0
                sp.wait_ge(qk_done, t + 1)
                sp.wait_ge(v_done, 2 * (t + 1))
                sp.dma_start(outs[0], ckvn[0:n, :]).then_inc(rows_out, 16)
                sp.dma_start(outs[1], rp9[0:n, 8, :]).then_inc(rows_out, 16)
                kf = Kk[0:n, H * KM:].rearrange("p (h d) -> p h d", h=H)
                sp.dma_start(outs[2].rearrange("t (h d) -> t h d", h=H), kf[:, :, 0:FD]).then_inc(rows_out, 16)
                sp.dma_start(outs[3], V[0:n, vb, 512:1024]).then_inc(rows_out, 16)
                sp.dma_start(outs[4], lf[0:n, b, :]).then_inc(rows_out, 16)
                if b == SBLK:
                    sp.dma_start(qs_dram, Qk[0:n, :]).then_inc(s_rows, 16)
                    sp.dma_start(ks_dram, Kk[0:n, :]).then_inc(s_rows, 16)
                    sp.dma_start(vs_dram, V[0:n, 0, 512:1024]).then_inc(s_rows, 16)
                    sp.dma_start(cs_dram, ckvn[0:n, :]).then_inc(s_rows, 16)
                if b == NB - 1:
                    for c in range(DC):
                        sp.dma_start(wq[:, c, :], w_q[:, c, :]).then_inc(wq_in, 16)
                    for c in range(3):
                        sp.dma_start(wo[:, c, :], w_o[:, c, :]).then_inc(wo_in, 16)
            sp.wait_ge(x_tr, NB + 1)
            sp.dma_start(hb[:, :], x_prompt[0:P, :]).then_inc(x_in, 16)
            sp.wait_ge(rows_out, 80 * (NB + 1))
            sp.wait_ge(qk_ps, 8 * NB)
            sp.dma_start(skT, sub_keys).then_inc(sk_in, 16)
            sp.wait_ge(o_ps, 16 * NB)
            for c in range(3, DC):
                sp.dma_start(wo[:, c, :], w_o[:, c, :]).then_inc(wo_in, 16)
            for b in range(NB):
                if b:
                    sp.wait_ge(q_ps, 4 * b)
                    sp.dma_start(hb[:, :], x_prompt[b * P:(b + 1) * P, :]).then_inc(x_in, 16)
                sp.wait_ge(h_made, b + 1)
                sp.dma_start(h_dram[b * P:(b + 1) * P, :], hb[:, :]).then_inc(h_stored, 16)
            sp.wait_ge(sc_done, 4 * NB)
            sp.dma_start(dcon, dec_consts).then_inc(dec_in, 16)
            sp.dma_start(wkd, w_k).then_inc(dec_in, 16)
            sp.dma_start(wkTd, w_kT).then_inc(dec_in, 16)
            sp.dma_start(SB[0:BD, 0:QW], qs_dram).then_inc(dec_in, 16)
            sp.dma_start(SA[0:BD, 0:QW], ks_dram).then_inc(dec_in, 16)
            sp.dma_start(prow, page_rows).then_inc(dec_in, 16)
            sp.wait_ge(const2_in, 16 * 4)

            def load_unit(i, par, keys):
                for j in range(4):
                    pg = sp.value_load(ptab[0:1, bass.ds(i * 8 + (par * 4 + j), 1)], min_val=0,
                                       max_val=kt_pool.shape[0] - 1)
                    src = kt_pool if keys else vn_pool
                    sp.dma_start(kbuf[:, par, j, :], src[bass.ds(pg, 1), :, :]
                                 .rearrange("a p n -> p (a n)")).then_inc(k_in[par], 16)
                    if keys:
                        sp.dma_start(kpb[0:RP, par, j, :], kpe_pool[bass.ds(pg, 1), :, :]
                                     .rearrange("a p n -> p (a n)")).then_inc(k_in[par], 16)

            for par in range(2):
                load_unit(0, par, True)
            with sp.Fori(1, NPG) as i:
                for par in range(2):
                    sp.wait_ge(k_used, sp.snap(2 * i + (par - 1)))
                    sp.sem_inc(sync_waited, 1)
                    load_unit(i, par, True)
            sp.wait_ge(abr_done, NPG + 2)
            sp.dma_start(sqd[0:BD, 0, :], vs_dram).then_inc(v_in, 16)
            sp.dma_start(sqd[0:BD, 1, 0:R], cs_dram).then_inc(v_in, 16)
            sp.dma_start(wvs, w_v).then_inc(v_in, 16)
            sp.wait_ge(soft_exp, 1)
            sp.wait_ge(top_done, NB)
            for c in range(DC):
                sp.dma_start(wo_s[:, c, :], w_o[:, c, :]).then_inc(swo_in, 16)
            for c in (0, 1, 2, 7):
                sp.dma_start(wq_s[c], w_q[:, c, :]).then_inc(swq_in, 16)
            with sp.Fori(0, NPG) as i:
                for par in range(2):
                    sp.wait_ge(k_used, sp.snap(2 * i + (2 * NPG + par - 1)))
                    sp.sem_inc(sync_waited, 1)
                    load_unit(i, par, False)
            sp.wait_ge(k_used, 4 * NPG)
            sp.dma_start(hs[0:BD, :], x_sample).then_inc(sx_in, 16)
            for c in (3, 4, 5, 6):
                sp.dma_start(wq_s[c], w_q[:, c, :]).then_inc(swq_in, 16)
            sp.wait_ge(u_used, P * NB)
            sp.dma_start(skT_s, sub_keys).then_inc(ssk_in, 16)
            sp.wait_ge(rows_out, 80 * (NB + 1))
            sp.wait_ge(h_stored, 16 * NB)
            sp.wait_ge(stored, 16 * (NB + 1))

        @block.gpsimd
        def _(pool):
            def gather(table, index, q):
                pool.indirect_dma_start(ring[:, q % RING, :], None, table,
                                        bass.IndirectOffsetOnAxis(ap=index, axis=0)).then_inc(g[q % RING], 16)

            pool.wait_ge(rows_out, 80 * (NB + 1))
            pool.wait_ge(s_rows, 64)
            def gather_logf(i):
                if i == 0:
                    pool.wait_ge(lg_in, 1)
                pool.indirect_dma_start(LG[:, i * P:(i + 1) * P], None, logf_pool,
                                        bass.IndirectOffsetOnAxis(ap=lgi[:, i:i + 1], axis=0)
                                        ).then_inc(lg_gathered, 16)

            for b in range(NB):
                pool.wait_ge(top_done, b + 1)
                for k in range(SLOTS):
                    if b == 2 and k % (SLOTS // NPG) == 0:
                        gather_logf(k // (SLOTS // NPG))
                    if b:
                        pool.wait_ge(v_used, P * b + min(k - RING + 1, 0))
                    ahead = U_AHEAD[b] if RING <= k < U_LAST[b] else RING
                    if k >= ahead:
                        pool.wait_ge(u_used, P * b + k - ahead + 1)
                    gather(peer_u, eidx[:, k:k + 1], 2 * P * b + k)
                pool.wait_ge(idxT_done, b + 1)
                for k in range(P):
                    if k >= RING:
                        pool.wait_ge(v_used, P * b + k - RING + 1)
                    else:
                        pool.wait_ge(u_used, P * (b + 1) + k - RING + 1)
                    gather(peer_v, idxT[:, gcol(k):gcol(k) + 1], 2 * P * b + P + k)
            pool.wait_ge(idxT_done, NB + 1)
            for k in range(BD):
                pool.wait_ge(v_used, P * NB + k - RING + 1)
                gather(peer_u, idxS[:, k:k + 1], 2 * P * NB + k)
            for k in range(BD):
                pool.wait_ge(s_u, k + 1)
                gather(peer_v, idxS[:, k:k + 1], 2 * P * NB + BD + k)

        @block.scalar
        def _(act):
            steps = [0, 0, 0]

            def step(ins):
                steps[0] += 1
                ins.then_inc(a_step, 1)
                act.wait_ge(a_step, steps[0])

            def rms(n, k):
                steps[1] += 1
                act.wait_ge(rms_in, steps[1])
                step(nc.scalar.activation(lnv[0:n, 0:k], ssv[0:n, 0:k], ACT.Ln))
                nc.scalar.activation(r0v[0:n, 0:k], lnv[0:n, 0:k], ACT.Exp, scale=-0.5).then_inc(rms_out, 1)

            def x_squares(t):
                m = ROWS[ORDER[t]]
                act.wait_ge(x_in, 16 * (t + 1))
                if t > 1:
                    act.wait_ge(proj_ps, 5 * t)
                junk = (sq if t < 2 else xnT_flat)[0:m, 0:D]
                nc.scalar.activation(junk, hb[0:m, :], ACT.Square, accum_out=ssa[0:m, 0:1]).then_inc(sumsq, 1)

            for t in range(2):
                x_squares(t)
                rms(ROWS[ORDER[t]], 1)
            for t, b in enumerate(ORDER):
                n = ROWS[b]
                vb = b if b < NB else 0
                for k, i in enumerate(PROJ_ORDER):
                    if i == 3:
                        continue
                    act.wait_ge(proj_ps, 5 * t + k + 1)
                    if k == 0:
                        act.wait_ge(rms_out, steps[1])
                    o = min(i, 3) * 512
                    m = 512 if i < 4 else 416
                    last = nc.scalar.activation(sq[0:n, o:o + m], ps[0:n, i, 0:m], ACT.Square)
                last.then_inc(sq_done, 1)
                if b == 0:
                    act.wait_ge(rows_out, 80)
                    act.wait_ge(s_rows, 64)
                nc.scalar.activation(V[0:n, vb, 512:1024], ps[0:n, 3, :], ACT.Copy).then_inc(v_done, 1)
                rms(n, 34)
                act.wait_ge(fz_done, t + 1)
                step(nc.scalar.activation(fz[0:n, 2, :], fz[0:n, 1, :], ACT.Exp, scale=-1.0))
                nc.scalar.activation(fz[0:n, 3, :], fz[0:n, 2, :], ACT.Ln, bias=1.0).then_inc(fexp_done, 1)
                act.wait_ge(ckv_ps, t + 1)
                nc.scalar.activation(ckvT[:, 0:n], ps[:, 7, 0:n], ACT.Copy).then_inc(ckvT_done, 1)
                act.wait_ge(kv_ps, t + 1)
                nc.scalar.activation(sq[0:n, 0:512], ps[0:n, 5, :], ACT.Square).then_inc(sq_done, 1)
                nc.scalar.activation(V[0:n, vb, 0:512], ps[0:n, 6, :], ACT.Copy).then_inc(v_done, 1)
                act.wait_ge(rp_done, t + 1)
                q3 = Qk[0:n, 0:H * KM].rearrange("p (h d) -> p h d", h=H)
                k3 = Kk[0:n, 0:H * KM].rearrange("p (h d) -> p h d", h=H)
                nc.scalar.activation(q3[:, :, NOPE:KM], rp9[0:n, 0:8, :], ACT.Copy)
                nc.scalar.activation(k3[:, :, NOPE:KM], rp9[0:n, 8:9, :].to_broadcast([n, H, RP]),
                                     ACT.Copy).then_inc(rp_copied, 1)
                rms(n, 8)
                if b == SBLK:
                    continue
                for gi in range(0, 8, 2):
                    act.wait_ge(qk_ps, 8 * b + gi + 1)
                    kd = KM if gi % 4 < 2 else KF
                    src = ps[0:kd, QKB[gi], :].rearrange("p (h t) -> p h t", h=4)
                    h0 = 4 * (gi % 4)
                    dst = QT[0:kd, h0:h0 + 4, :] if gi < 4 else KT[0:kd, h0:h0 + 4, b * P:(b + 1) * P]
                    nc.scalar.activation(dst, src, ACT.Copy).then_inc(qk_even, 1)
                w = (b + 1) * P

                def copy_pT(hh):
                    act.wait_ge(pT_ps, 16 * b + hh + 1)
                    if 16 * b + hh >= 2:
                        act.wait_ge(o_ps, 16 * b + hh - 1)
                    nc.scalar.activation(PT[:, hh % 2, 0:w], ps[:, 4 + hh % 2, 0:w],
                                         ACT.Copy).then_inc(pT_done[1], 1)

                for hh in range(16):
                    act.wait_ge(max_done, 16 * b + hh + 1)
                    if 16 * b + hh >= 2:
                        act.wait_ge(pT_ps, 16 * b + hh - 1)
                    nc.scalar.activation(Pm[:, hh % 2, 0:w], ps[:, 2 + hh % 2, 0:w], ACT.Exp,
                                         bias=nmx[:, hh:hh + 1], accum_out=rs[:, hh:hh + 1]
                                         ).then_inc(exp_done, 1)
                    if hh and (hh - 1) % 2:
                        copy_pT(hh - 1)
                    if t < NB and hh == 4:
                        x_squares(t + 1)
                    if t < NB and hh == 6:
                        rms(P, 1)
                copy_pT(15)
                act.wait_ge(mx_done, b + 1)
                act.wait_ge(o_ps, 16 * (b + 1))
                for i in range(2):
                    last = nc.scalar.activation(sq[:, i * 512:(i + 1) * 512], mx[:, i * 512:(i + 1) * 512],
                                                ACT.Square, accum_out=ssa[:, 1 + i:2 + i])
                last.then_inc(sumsq, 1)
                rms(P, 2)

            def gate_exp(b):
                n = ROWS[b]
                act.wait_ge(gexp_in, b + 1)
                nc.scalar.activation(gate[0:n, b % 2, :], gate[0:n, b % 2, :], ACT.Exp).then_inc(gexp_out, 1)

            for b in range(NB):
                if b == 1:
                    gate_exp(0)
                act.wait_ge(h_made, b + 1)
                nc.scalar.activation(xn2[:, b, :], hb[:, :], ACT.Square, accum_out=ssa[:, 3:4]).then_inc(sumsq, 1)
                rms(P, 1)
                act.wait_ge(tr_ps, b + 1)
                act.wait_ge(h_stored, 16 * (b + 1))
                for i in range(2):
                    last = nc.scalar.activation(hb[:, i * 512:(i + 1) * 512], ps[:, 6 + i, :], ACT.Copy)
                last.then_inc(xnT2_done, 1)

                def copy_queries(i):
                    act.wait_ge(q_ps, 4 * b + i + 1)
                    if b:
                        act.wait_ge(sc_ps, 4 * b - 3 + i)
                    nc.scalar.activation(qpT[:, 4 * i:4 * i + 4, :], ps[:, 2 + i, :]
                                         .rearrange("p (g t) -> p g t", g=4), ACT.Copy).then_inc(q_done, 1)

                def copy_scores(i):
                    act.wait_ge(sc_ps, 4 * b + i + 1)
                    if b == 3 and i == 0:
                        act.wait_ge(top_done, 1)
                    nc.scalar.activation(sc[:, b % 3, 4 * i:4 * i + 4, :], ps[:, SCB[i], :]
                                         .rearrange("p (g t) -> p g t", g=4), ACT.Copy).then_inc(sc_done, 1)

                copy_queries(0)
                for i in range(1, 4):
                    copy_queries(i)
                    copy_scores(i - 1)
                copy_scores(3)

            def gelu(b):
                act.wait_ge(u_used, P * (b + 1))
                nc.scalar.activation(acc[:, :], acc[:, :], ACT.Gelu).then_inc(gelu_done, 1)

            def load_h(b):
                if b:
                    act.wait_ge(stored, 16 * b)
                else:
                    act.wait_ge(q_ps, 4 * NB)
                act.dma_start(hb[:, :], h_dram[b * P:(b + 1) * P, :]).then_inc(h_in, 16)

            def store_y(b):
                act.wait_ge(y_done, b + 1)
                act.dma_start(y_prompt[b * P:(b + 1) * P, :], hb[:, :]).then_inc(stored, 16)

            def decode_scores(first, last_it):
                with act.Fori(first, last_it) as it:
                    for s in range(2):
                        for par in range(2):
                            for q in range(4):
                                m = (2 * s + par) * 4 + q
                                act.wait_ge(n_ps, act.snap(it * 16 + (m + 1)))
                                act.sem_inc(scalar_waited, 1)
                                act.wait_ge(sqd_used, act.snap(it * 16 + (m + 1)))
                                nc.scalar.activation(sqd[:, q % 2, :], ps[:, 2 + q % 2, :],
                                                     ACT.Square).then_inc(sqd_done, 1)
                        act.wait_ge(sqd_used, act.snap(it * 16 + (8 * s + 10)))
                        act.sem_inc(scalar_waited, 1)
                        nc.scalar.activation(SABR[:, :, bass.ds(it * 256 + s * 128, 128)],
                                             ps[:, 4 + s, 0:3 * P].rearrange("p (k n) -> p k n", k=3),
                                             ACT.Copy).then_inc(abr_done, 1)

            gelu(0)
            load_h(0)
            act.wait_ge(dq_done, 1)
            act.wait_ge(d_ps, 1)
            nc.scalar.activation(qTd, ps[:, 6, 0:64].rearrange("p (c b) -> p c b", c=8), ACT.Copy)
            nc.scalar.activation(qpT8[0:RP], ps[0:RP, 6, 64:128].rearrange("p (c b) -> p c b", c=8),
                                 ACT.Copy).then_inc(d_sb, 1)
            act.sem_inc(sqd_done, 2)
            act.sem_inc(abr_done, 2)
            decode_scores(0, 1)
            gate_exp(1)
            store_y(0)
            decode_scores(1, 8)
            gelu(1)
            load_h(1)
            decode_scores(8, 9)
            gate_exp(2)
            store_y(1)
            decode_scores(9, 16)
            gelu(2)
            load_h(2)
            gate_exp(3)
            act.wait_ge(soft_in, 1)
            step(nc.scalar.activation(kscr, SR, ACT.Ln))
            nc.scalar.activation(kscr, kscr, ACT.Exp, scale=-0.5).then_inc(soft_ln, 1)
            act.wait_ge(soft_max, 1)
            nc.scalar.activation(SA, SA, ACT.Exp, bias=dsm[:, 34:35], accum_out=dsm[:, 36:37])
            nc.scalar.activation(dsm[:, 35:36], dsm[:, 32:33], ACT.Exp, bias=dsm[:, 34:35]).then_inc(soft_exp, 1)
            store_y(2)
            act.sem_inc(pd_done, 2)
            with act.Fori(0, NPG // 2) as it:
                for s in range(2):
                    act.wait_ge(pd_ps, act.snap(it * 2 + (s + 2)))
                    act.sem_inc(scalar_waited, 1)
                    nc.scalar.activation(stg[:, s, :], SA[:, bass.ds(it * 256 + s * 128, 128)],
                                         ACT.Copy).then_inc(stg_done, 1)
                    act.wait_ge(pd_ps, act.snap(it * 2 + (s + 4)))
                    act.sem_inc(scalar_waited, 1)
                    act.wait_ge(k_used, act.snap(it * 4 + (2 * NPG - 2 + 2 * s)))
                    nc.scalar.activation(pTd[:, s, :], ps[:, 2 + s, 0:P],
                                         ACT.Copy).then_inc(pd_done, 1)
            gelu(3)
            load_h(3)
            act.wait_ge(oLT_ps, 1)
            nc.scalar.activation(oLT, ps[:, 7, 0:P], ACT.Copy).then_inc(s_sum, 1)
            act.wait_ge(dm_done, 1)
            step(nc.scalar.activation(oX[0:BD, 0:512], mxs[0:BD, 0:512], ACT.Square, accum_out=ssa[0:BD, 1:2]))
            nc.scalar.activation(oX[0:BD, 0:512], mxs[0:BD, 512:1024], ACT.Square,
                                 accum_out=ssa[0:BD, 2:3]).then_inc(sumsq, 1)
            rms(BD, 2)
            act.wait_ge(s_h, 1)
            nc.scalar.activation(mxs[0:BD, :], hs[0:BD, :], ACT.Square, accum_out=ssa[0:BD, 3:4]).then_inc(sumsq, 1)
            rms(BD, 1)
            act.wait_ge(s_tr, 2)
            nc.scalar.activation(xTs, ps[:, 7, 0:64].rearrange("p (c t) -> p c t", c=DC), ACT.Copy).then_inc(s_xT, 1)
            act.wait_ge(s_q, 1)
            for j in range(4):
                last = nc.scalar.activation(qrow[32 * j:32 * j + BD, :], ps[32 * j:32 * j + BD, 6, :], ACT.Copy)
            last.then_inc(s_qr, 1)
            act.wait_ge(s_qt, 1)
            nc.scalar.activation(qTs.rearrange("p (j m) t -> p m j t", j=4),
                                 ps[:, 7, :].rearrange("p (m j t) -> p m j t", m=4, j=4)[:, :, :, 0:BD],
                                 ACT.Copy).then_inc(s_qT, 1)
            gate_exp(4)
            store_y(3)
            act.wait_ge(s_u, BD)
            nc.scalar.activation(acc[:, 0:BD], acc[:, 0:BD], ACT.Gelu).then_inc(gelu_done, 1)
            act.wait_ge(y_done, NB + 1)
            act.dma_start(y_sample, hs[0:BD, :]).then_inc(stored, 16)

        @block.vector
        def _(dve):
            count = {"step": 0, "rms": 0, "ssq": 0, "sq": 0}
            V_ = nc.vector

            def after(ins):
                count["step"] += 1
                ins.then_inc(v_step, 1)
                return count["step"]

            def step(ins):
                dve.wait_ge(v_step, after(ins))

            def rms(n, k):
                count["rms"] += 1
                dve.wait_ge(rms_out, count["rms"])
                step(V_.tensor_tensor(tv[0:n, 0:k], r0v[0:n, 0:k], r0v[0:n, 0:k], ALU.mult))
                step(V_.tensor_tensor(tv[0:n, 0:k], tv[0:n, 0:k], ssv[0:n, 0:k], ALU.mult))
                step(V_.tensor_scalar(tv[0:n, 0:k], tv[0:n, 0:k], -0.5, 1.5, ALU.mult, ALU.add))
                step(V_.tensor_tensor(rv[0:n, 0:k], tv[0:n, 0:k], r0v[0:n, 0:k], ALU.mult))

            def rms_of(n, src, dim):
                count["ssq"] += 1
                dve.wait_ge(sumsq, count["ssq"])
                V_.tensor_scalar(ssv[0:n, 0:src.shape[1]], src, 1.0 / dim, EPS, ALU.mult, ALU.add).then_inc(rms_in, 1)
                rms(n, src.shape[1])

            def heads(ap, n, h=H):
                return ap.rearrange("p (h d) -> p h d", h=h)

            def bc(ap, n, h, d):
                return ap.unsqueeze(2).to_broadcast([n, h, d])

            def gb(a, n, h, d):
                return gs[0:n, a:a + d].unsqueeze(1).to_broadcast([n, h, d])

            dve.wait_ge(const_in, 16 * 3)
            q3f = Qk[:, H * KM:].rearrange("p (h d) -> p h d", h=H)
            k3f = Kk[:, H * KM:].rearrange("p (h d) -> p h d", h=H)
            V_.memset(q3f[:, :, FD:FD + 1], 1.0)
            step(V_.memset(k3f[:, :, FD + 1:FD + 2], 1.0))

            def x_mean(t):
                m = ROWS[ORDER[t]]
                count["ssq"] += 1
                dve.wait_ge(sumsq, count["ssq"])
                V_.tensor_scalar(ssv[0:m, 0:1], ssa[0:m, 0:1], 1.0 / D, EPS, ALU.mult, ALU.add).then_inc(rms_in, 1)

            def x_scale(t):
                m = ROWS[ORDER[t]]
                rms(m, 1)
                V_.tensor_scalar(hb[0:m, :], hb[0:m, :], rv[0:m, 0:1], None, ALU.mult).then_inc(x_norm, 1)

            def x_gain(t):
                m = ROWS[ORDER[t]]
                dve.wait_ge(x_tr, t + 1)
                for i in range(2):
                    last = V_.tensor_tensor(xnT[:, 4 * i:4 * i + 4, 0:m],
                                            ps[:, 6 + i, 0:4 * m].rearrange("p (c t) -> p c t", c=4),
                                            gT[:, 4 * i:4 * i + 4].unsqueeze(2).to_broadcast([P, 4, m]), ALU.mult)
                last.then_inc(xnT_done, 1)

            x_mean(0)
            x_scale(0)
            x_gain(0)
            x_mean(1)
            x_scale(1)
            for t, b in enumerate(ORDER):
                n = ROWS[b]
                count["sq"] += 1
                dve.wait_ge(sq_done, count["sq"])
                if t == 0:
                    x_gain(1)
                for i in range(3):
                    V_.tensor_reduce(ssv[0:n, 8 * i:8 * i + 8], heads(sq[0:n, 512 * i:512 * i + 512], n),
                                     AX.X, ALU.add)
                V_.tensor_reduce(ssv[0:n, 24:32], heads(sq[0:n, 1536:1792], n), AX.X, ALU.add)
                V_.tensor_reduce(ssv[0:n, 32:33], sq[0:n, 1792:1920], AX.X, ALU.add)
                step(V_.tensor_reduce(ssv[0:n, 33:34], sq[0:n, 1920:1952], AX.X, ALU.add))
                step(V_.tensor_tensor(ssv[0:n, :], ssv[0:n, :], con[0:n, C_DIM:C_DIM + 34], ALU.mult))
                V_.tensor_scalar(ssv[0:n, :], ssv[0:n, :], EPS, None, ALU.add).then_inc(rms_in, 1)
                step(V_.tensor_tensor(fz[0:n, 0, :], ps[0:n, 4, TAIL_F:TAIL], gs[0:n, G_BF:G_BF + H], ALU.add))
                V_.scalar_tensor_tensor(fz[0:n, 1, :], fz[0:n, 0, :], -1.0, fz[0:n, 0, :], ALU.mult,
                                        ALU.max).then_inc(fz_done, 1)
                rms(n, 34)
                if t:
                    dve.wait_ge(rows_out, 80 * t)
                if t == 1:
                    dve.wait_ge(s_rows, 64)
                V_.scalar_tensor_tensor(ckvn[0:n, :], ps[0:n, 4, TAIL_CKV:TAIL_KPE], rv[0:n, 32:33],
                                        gs[0:n, G_CKV:G_CKV + R], ALU.mult, ALU.mult).then_inc(ckv_done, 1)
                V_.tensor_scalar(rv[0:n, 0:8], rv[0:n, 0:8], S_MLA, None, ALU.mult)
                V_.tensor_scalar(rv[0:n, 8:16], rv[0:n, 8:16], S_FOX, None, ALU.mult)
                step(V_.tensor_scalar(rv[0:n, 24:32], rv[0:n, 24:32], S_MLA, None, ALU.mult))
                q3 = heads(Qk[0:n, 0:H * KM], n)
                k3 = heads(Kk[0:n, 0:H * KM], n)
                V_.tensor_tensor(pe9[0:n, 0:8, :], heads(ps[0:n, 4, 0:256], n), bc(rv[0:n, 24:32], n, H, RP), ALU.mult)
                V_.tensor_scalar(pe9[0:n, 8, :], ps[0:n, 4, TAIL_KPE:TAIL_F], rv[0:n, 33:34], None, ALU.mult)
                V_.tensor_tensor(q3[:, :, 0:NOPE], heads(ps[0:n, 0, :], n), bc(rv[0:n, 0:8], n, H, NOPE), ALU.mult)
                V_.tensor_tensor(q3f[0:n, :, 0:FD], heads(ps[0:n, 1, :], n), bc(rv[0:n, 8:16], n, H, FD), ALU.mult)
                step(V_.tensor_tensor(k3f[0:n, :, 0:FD], heads(ps[0:n, 2, :], n), bc(rv[0:n, 16:24], n, H, FD), ALU.mult))
                V_.tensor_tensor(pe9[0:n, 0:8, :], pe9[0:n, 0:8, :], gb(G_QPE, n, H, RP), ALU.mult)
                V_.tensor_tensor(pe9[0:n, 8, :], pe9[0:n, 8, :], gs[0:n, G_KPE:G_KPE + RP], ALU.mult)
                V_.tensor_tensor(q3[:, :, 0:NOPE], q3[:, :, 0:NOPE], gb(G_QN, n, H, NOPE), ALU.mult)
                V_.tensor_tensor(q3f[0:n, :, 0:FD], q3f[0:n, :, 0:FD], gb(G_FQ, n, H, FD), ALU.mult)
                step(V_.tensor_tensor(k3f[0:n, :, 0:FD], k3f[0:n, :, 0:FD], gb(G_FK, n, H, FD), ALU.mult))
                cos = con[0:n, C_COS + 16 * b:C_COS + 16 * b + 16].unsqueeze(1).to_broadcast([n, 9, 16])
                sin = con[0:n, C_SIN + 16 * b:C_SIN + 16 * b + 16].unsqueeze(1).to_broadcast([n, 9, 16])
                x1, x2 = pe9[0:n, :, 0:16], pe9[0:n, :, 16:32]
                V_.tensor_tensor(rt[0:n, 0], x1, cos, ALU.mult)
                step(V_.tensor_tensor(rt[0:n, 1], x2, sin, ALU.mult))
                step(V_.tensor_tensor(rp9[0:n, :, 0:16], rt[0:n, 0], rt[0:n, 1], ALU.subtract))
                V_.tensor_tensor(rt[0:n, 0], x1, sin, ALU.mult)
                step(V_.tensor_tensor(rt[0:n, 1], x2, cos, ALU.mult))
                V_.tensor_tensor(rp9[0:n, :, 16:32], rt[0:n, 0], rt[0:n, 1], ALU.add).then_inc(rp_done, 1)
                dve.wait_ge(fexp_done, t + 1)
                V_.scalar_tensor_tensor(lf[0:n, b, :], fz[0:n, 0, :], 0.0, fz[0:n, 3, :], ALU.min,
                                        ALU.subtract).then_inc(lf_done, 1)
                count["sq"] += 1
                dve.wait_ge(sq_done, count["sq"])
                step(V_.tensor_reduce(ssv[0:n, 0:8], heads(sq[0:n, 0:512], n), AX.X, ALU.add))
                V_.tensor_scalar(ssv[0:n, 0:8], ssv[0:n, 0:8], 1.0 / NOPE, EPS, ALU.mult, ALU.add).then_inc(rms_in, 1)
                rms(n, 8)
                step(V_.tensor_tensor(k3[:, :, 0:NOPE], heads(ps[0:n, 5, :], n), bc(rv[0:n, 0:8], n, H, NOPE), ALU.mult))
                step(V_.tensor_tensor(k3[:, :, 0:NOPE], k3[:, :, 0:NOPE], gb(G_KN, n, H, NOPE), ALU.mult))
                if b == SBLK:
                    dve.wait_ge(rp_copied, t + 1)
                    V_.memset(q3f[0:n, :, FD + 1:FD + 2], 0.0)
                    V_.memset(k3f[0:n, :, FD:FD + 1], 0.0).then_inc(qk_done, 1)
                    continue
                dve.wait_ge(c_ps, b + 1)
                cc = ps[:, 7, 256:256 + H].unsqueeze(2)
                V_.tensor_copy(q3f[:, :, FD + 1:FD + 2], cc)
                dve.wait_ge(rp_copied, t + 1)
                V_.tensor_scalar(k3f[:, :, FD:FD + 1], cc, -1.0, None, ALU.mult).then_inc(qk_done, 1)
                for gi in range(1, 8, 2):
                    dve.wait_ge(qk_ps, 8 * b + gi + 1)
                    kd = KM if gi % 4 < 2 else KF
                    src = ps[0:kd, QKB[gi], :].rearrange("p (h t) -> p h t", h=4)
                    h0 = 4 * (gi % 4)
                    dst = QT[0:kd, h0:h0 + 4, :] if gi < 4 else KT[0:kd, h0:h0 + 4, b * P:(b + 1) * P]
                    V_.tensor_copy(dst, src).then_inc(qk_odd, 1)
                w = (b + 1) * P

                def copy_pT(hh):
                    dve.wait_ge(pT_ps, 16 * b + hh + 1)
                    if 16 * b + hh >= 2:
                        dve.wait_ge(o_ps, 16 * b + hh - 1)
                    V_.tensor_copy(PT[:, hh % 2, 0:w], ps[:, 4 + hh % 2, 0:w]).then_inc(pT_done[0], 1)

                for hh in range(16):
                    dve.wait_ge(s_ps, 16 * b + hh + 1)
                    step(V_.tensor_tensor(ps[:, 2 + hh % 2, b * P:w], ps[:, 2 + hh % 2, b * P:w],
                                          con[:, C_MASK:C_MASK + P], ALU.add))
                    V_.tensor_reduce(nmx[:, hh:hh + 1], ps[:, 2 + hh % 2, 0:w], AX.X, ALU.max,
                                     negate=True).then_inc(max_done, 1)
                    if hh and (hh - 1) % 2 == 0:
                        copy_pT(hh - 1)
                    if t < NB and hh == 5:
                        x_mean(t + 1)
                    if t < NB and hh == 7:
                        x_scale(t + 1)
                    if t < NB and hh == 12:
                        x_gain(t + 1)
                dve.wait_ge(o_ps, 16 * (b + 1))
                step(V_.reciprocal(rs[:, :], rs[:, :]))
                V_.tensor_tensor(heads(mx[:, 0:512], P), heads(ps[:, 0, :], P), bc(rs[:, 0:8], P, H, VD), ALU.mult)
                V_.tensor_tensor(heads(mx[:, 512:1024], P), heads(ps[:, 1, :], P), bc(rs[:, 8:16], P, H, VD),
                                 ALU.mult).then_inc(mx_done, 1)
                rms_of(P, ssa[:, 1:3], 512)
                V_.tensor_scalar(mx[:, 0:512], mx[:, 0:512], rv[:, 0:1], None, ALU.mult)
                V_.tensor_scalar(mx[:, 512:1024], mx[:, 512:1024], rv[:, 1:2], None, ALU.mult).then_inc(m_norm, 1)
                dve.wait_ge(m_tr, b + 1)
                for i in range(2):
                    last = V_.tensor_tensor(mixT[:, b, 4 * i:4 * i + 4, :],
                                            ps[:, 6 + i, :].rearrange("p (c t) -> p c t", c=4),
                                            gT[:, DC + 4 * i:DC + 4 * i + 4].unsqueeze(2).to_broadcast([P, 4, P]),
                                            ALU.mult)
                last.then_inc(mixT_done, 1)

            dve.wait_ge(const2_in, 16 * 4)

            def norm2(b):
                dve.wait_ge(op_ps, b + 1)
                dve.wait_ge(x_in, 16 * (NB + 1 + b + 1))
                for i in range(2):
                    last = V_.tensor_tensor(hb[:, i * 512:(i + 1) * 512], ps[:, i, :],
                                            hb[:, i * 512:(i + 1) * 512], ALU.add)
                last.then_inc(h_made, 1)
                rms_of(P, ssa[:, 3:4], D)
                V_.scalar_tensor_tensor(xn2[:, b, :], hb[:, :], rv[:, 0:1], gf[:, :], ALU.mult,
                                        ALU.mult).then_inc(xn2_done, 1)

            def top16_of_two(two):
                c = [after(V_.max(v[:, 0:8], src)) for v, _, src, _ in two]
                for i, (v, pos, src, rest) in enumerate(two):
                    dve.wait_ge(v_step, c[i])
                    c[i] = after(V_.max_index(pos[:, 0:8], v[:, 0:8], src))
                for i, (v, pos, src, rest) in enumerate(two):
                    dve.wait_ge(v_step, c[i])
                    c[i] = after(V_.match_replace(rest, v[:, 0:8], src, NEG))
                for i, (v, pos, src, rest) in enumerate(two):
                    dve.wait_ge(v_step, c[i])
                    c[i] = after(V_.max(v[:, 8:16], rest))
                for i, (v, pos, src, rest) in enumerate(two):
                    dve.wait_ge(v_step, c[i])
                    c[i] = after(V_.max_index(pos[:, 8:16], v[:, 8:16], rest))
                dve.wait_ge(v_step, c[1])

            def top_subkeys(b, scores, lo, hi):
                n = ROWS[b]
                for hp in range(lo, hi, 2):
                    top16_of_two([(topv[0:n, hp + i, :], topi[0:n, hp + i, :], scores(hp + i),
                                   mrep[0:n, i * P:(i + 1) * P]) for i in range(2)])

            def top_experts(b):
                n = ROWS[b]
                big = sc[0:n, b % 3, :, :].rearrange("p g k -> p (g k)")
                b4 = big.rearrange("p (h a c) -> p h a c", h=PHEADS, a=TOPK)
                b3 = big.rearrange("p (x a) -> p x a", a=TOPK)
                v4 = topv[0:n].rearrange("p (h i) k -> p h i k", i=2)
                f4 = topf[0:n].rearrange("p (h i) k -> p h i k", i=2)
                at = topi[0:n].rearrange("p a b -> p (a b)")
                pos, hi = at[:, 0:SLOTS], at[:, SLOTS:2 * SLOTS]
                fpos = mrep[0:n, :].rearrange("p (i x) -> p i x", i=2)
                iota = con[0:n, C_IOTA:C_IOTA + TOPK].unsqueeze(1).to_broadcast([n, SLOTS, TOPK])
                all4 = [n, PHEADS, TOPK, TOPK]
                if b:
                    dve.wait_ge(idx_ps, b)
                V_.tensor_copy(topf[0:n], topi[0:n])
                step(V_.tensor_tensor(b4, v4[:, :, 0, :].unsqueeze(3).to_broadcast(all4),
                                      v4[:, :, 1, :].unsqueeze(2).to_broadcast(all4), ALU.add))
                for h in range(0, PHEADS, 2):
                    top16_of_two([(gate[0:n, b % 2, TOPK * k:TOPK * (k + 1)], pos[:, TOPK * k:TOPK * (k + 1)],
                                   big[:, 256 * k:256 * (k + 1)], big[:, 256 * k:256 * (k + 1)])
                                  for k in (h, h + 1)])
                step(V_.tensor_scalar(hi, pos, 4, None, ALU.logical_shift_right))
                V_.tensor_copy(fpos[:, 0, :], hi)
                step(V_.tensor_scalar(pos, pos, 15, None, ALU.bitwise_and))
                step(V_.tensor_copy(fpos[:, 1, :], pos))
                for i, dst in enumerate((eidf[0:n, :], fpos[:, 0, :])):
                    step(V_.tensor_tensor(b3, fpos[:, i, :].unsqueeze(2).to_broadcast([n, SLOTS, TOPK]), iota,
                                          ALU.is_equal))
                    step(V_.tensor_tensor(b4, b4, f4[:, :, i, :].unsqueeze(2).to_broadcast(all4), ALU.mult))
                    step(V_.tensor_reduce(dst, b3, AX.X, ALU.add))
                step(V_.scalar_tensor_tensor(eidf[0:n, :], eidf[0:n, :], float(P), fpos[:, 0, :], ALU.mult, ALU.add))
                V_.tensor_copy(eidx[0:n, :], eidf[0:n, :]).then_inc(top_done, 1)
                g3 = gate[0:n, b % 2, :].rearrange("p (h k) -> p h k", h=PHEADS)
                step(V_.tensor_copy(fz[0:n, 0, :].unsqueeze(2), g3[:, :, 0:1]))
                V_.tensor_tensor(g3, g3, bc(fz[0:n, 0, :], n, PHEADS, TOPK), ALU.subtract).then_inc(gexp_in, 1)
                dve.wait_ge(gexp_out, b + 1)
                step(V_.tensor_reduce(fz[0:n, 1, :], g3, AX.X, ALU.add))
                step(V_.reciprocal(fz[0:n, 2, :], fz[0:n, 1, :]))
                V_.tensor_tensor(g3, g3, bc(fz[0:n, 2, :], n, PHEADS, TOPK), ALU.mult).then_inc(gates_done, 1)
                dve.wait_ge(gates_done, b + 1)

            def scores_of(b):
                return lambda hp: sc[:, b % 3, hp, :]

            def copy_idxT(b):
                n = ROWS[b]
                dve.wait_ge(idx_ps, b + 1)
                V_.tensor_copy((idxT if b < NB else idxS)[:, 0:n], ps[:, 7, 0:n]).then_inc(idxT_done, 1)

            def decode_queries_1():
                dve.wait_ge(dec_in, 96)
                sc1 = SR[0:BD, 0:16 * KM]
                m3 = heads(sc1[:, 0:H * KM], BD)
                f3 = heads(sc1[:, H * KM:H * KM + 512], BD)
                qm, km = heads(SB[0:BD, 0:H * KM], BD), heads(SA[0:BD, 0:H * KM], BD)
                qf, kf = heads(SB[0:BD, H * KM:QW], BD), heads(SA[0:BD, H * KM:QW], BD)
                V_.tensor_tensor(m3, qm, km, ALU.mult)
                step(V_.tensor_tensor(f3, qf[:, :, 0:FD], kf[:, :, 0:FD], ALU.mult))
                V_.tensor_reduce(dsm[0:BD, 8:16], m3, AX.X, ALU.add)
                V_.tensor_reduce(dsm[0:BD, 0:8], f3, AX.X, ALU.add)
                V_.tensor_copy(dsm[0:BD, 16:24], lf[0:BD, SBLK, :])
                V_.memset(dsm[0:BD, 24:32], 0.0)
                V_.tensor_copy(heads(SR[0:BD, 2048:2560], BD), qf[:, :, 0:FD])
                V_.tensor_tensor(heads(SR[0:BD, 2560:3072], BD), qm[:, :, 0:NOPE], gb(G_KN, BD, H, NOPE), ALU.mult)
                V_.memset(qz, 0.0)
                V_.memset(qpz, 0.0)
                V_.memset(qbd, 0.0).then_inc(dq_done, 1)
                dve.wait_ge(dq_done, 1)
                for i in range(2):
                    m = dsm[0:BD, 64 + 128 * i:192 + 128 * i].rearrange("p (b r) -> p b r", b=BD)
                    last = V_.tensor_tensor(m, dcon[0:BD, E_BT:E_BT + P].rearrange("p (b r) -> p b r", b=BD),
                                            dsm[0:BD, 16 * i:16 * i + 16].unsqueeze(1).to_broadcast([BD, BD, 16]),
                                            ALU.mult)
                last.then_inc(dq_in, 1)

            def decode_queries_2():
                dve.wait_ge(d_sb, 1)
                for half in range(2):
                    hs_ = slice(64 * half, 64 * half + 64)
                    last = V_.tensor_copy(qbd[hs_, :, 8 * half:8 * half + 8], qTd[hs_, 4:8, :])
                last.then_inc(dq_in, 1)
                for half in range(2):
                    hs_ = slice(64 * half, 64 * half + 64)
                    for p2 in range(2):
                        for c in range(4):
                            m = 16 * p2 + 2 * c + half
                            V_.tensor_copy(qz[hs_, c, p2::2, m:m + 1], qTd[hs_, c, p2::2].unsqueeze(2))
                for p2 in range(2):
                    V_.tensor_copy(qpz[0:RP, p2::2, 16 * p2 + 8:16 * p2 + 16],
                                   qpT8[0:RP, :, p2::2].rearrange("p h j -> p j h"))
                dve.wait_ge(d_ps, 2)
                V_.tensor_copy(dsm[:, 32:34], ps[:, 6, 128:130])
                for q in range(4):
                    for half in range(2):
                        for p2 in range(2):
                            m = 16 * p2 + 8 + 2 * q + half
                            a = 256 + 16 * q + 8 * half
                            last = V_.tensor_copy(qz[:, 4, p2::2, m:m + 1],
                                                  ps[:, 6, a + p2:a + 8:2].unsqueeze(2))
                last.then_inc(dq_done, 1)

            def u_phase(b, between):
                for k in range(SLOTS):
                    if k % 8 == 0 and k // 8 in between:
                        for f in between[k // 8]:
                            f()
                    q = 2 * P * b + k
                    dve.wait_ge(g[q % RING], 16 * (q // RING + 1))
                    V_.tensor_tensor_reduce(ring[:, q % RING, :], ring[:, q % RING, :], xn2[:, b, :], 1.0, 0.0,
                                            ALU.mult, ALU.add, acc[:, k:k + 1]).then_inc(u_used, 1)
                dve.wait_ge(gelu_done, b + 1)
                V_.tensor_tensor(acc[:, :], acc[:, :], gate[:, b % 2, :], ALU.mult).then_inc(w_done, 1)
                dve.wait_ge(w_ps, b + 1)
                if b:
                    dve.wait_ge(v_used, P * b)
                V_.tensor_copy(Wd, ps[:, 7, 0:P].rearrange("p (j c) -> p j c", j=4)).then_inc(W_done, 1)

            def add_y(b):
                dve.wait_ge(v_used, P * (b + 1))
                dve.wait_ge(h_in, 16 * (b + 1))
                for i in range(2):
                    last = V_.tensor_tensor(hb[:, i * 512:(i + 1) * 512], ps[:, i, :],
                                            hb[:, i * 512:(i + 1) * 512], ALU.add)
                last.then_inc(y_done, 1)

            def zero_W():
                dve.wait_ge(sc_ps, 4 * NB)
                step(V_.memset(W32[:, :, :, :].rearrange("p j c m -> p (j c m)"), 0.0))

            norm2(0)
            for i in range(4):
                dve.wait_ge(sc_done, i + 1)
                top_subkeys(0, scores_of(0), 4 * i, 4 * i + 4)
            top_experts(0)
            norm2(1)
            u_phase(0, {6: [lambda: norm2(2)], 11: [lambda: norm2(3)], 15: [lambda: copy_idxT(0), zero_W]})
            decode_queries_1()
            decode_queries_2()
            top_subkeys(1, scores_of(1), 0, 16)
            top_experts(1)
            u_phase(1, {1: [lambda: add_y(0)], 2: [lambda: copy_idxT(1)]})
            top_subkeys(2, scores_of(2), 0, 16)
            top_experts(2)
            step(V_.tensor_copy(lgf, prow))
            step(V_.tensor_scalar(lgf, lgf, 16.0, dcon[:, E_MOD:E_MOD + 1], ALU.mult, ALU.add))
            V_.tensor_copy(lgi, lgf).then_inc(lg_in, 1)
            u_phase(2, {1: [lambda: add_y(1)], 2: [lambda: copy_idxT(2)]})
            top_subkeys(3, scores_of(3), 0, 16)
            top_experts(3)
            dve.wait_ge(abr_done, NPG + 2)
            V_.tensor_scalar(SR, SR, 1.0 / NOPE, EPS, ALU.mult, ALU.add).then_inc(soft_in, 1)
            dve.wait_ge(soft_ln, 1)
            V_.tensor_tensor(SB, SB, kscr, ALU.mult)
            step(V_.tensor_tensor(SR, SR, kscr, ALU.mult))
            step(V_.tensor_tensor(SR, SR, kscr, ALU.mult))
            step(V_.tensor_scalar(SR, SR, -0.5, 1.5, ALU.mult, ALU.add))
            step(V_.tensor_tensor(SB, SB, SR, ALU.mult))
            step(V_.tensor_tensor(SA, SA, SB, ALU.add))
            dve.wait_ge(lg_gathered, 16 * NPG)
            step(V_.tensor_tensor_scan(SB, con[:, C_ONES:C_ONES + 1].to_broadcast([P, PAST]), LG, 0.0,
                                       ALU.mult, ALU.add))
            step(V_.tensor_tensor(dsm[:, 37:38], SB[:, PAST - 1:PAST], dsm[:, 33:34], ALU.add))
            step(V_.tensor_scalar(SB, SB, dsm[:, 37:38], -1.0, ALU.subtract, ALU.mult))
            step(V_.tensor_tensor(SA, SA, SB, ALU.add))
            step(V_.tensor_reduce(dsm[:, 38:39], SA, AX.X, ALU.max))
            step(V_.tensor_tensor(dsm[:, 38:39], dsm[:, 38:39], dsm[:, 32:33], ALU.max))
            V_.tensor_scalar(dsm[:, 34:35], dsm[:, 38:39], -1.0, None, ALU.mult).then_inc(soft_max, 1)
            dve.wait_ge(soft_exp, 1)
            V_.tensor_scalar(dsm[:, 48:56], dcon[:, E_B:E_B + BD], dsm[:, 35:36], None, ALU.mult).then_inc(dq_done, 1)
            step(V_.tensor_tensor(dsm[:, 39:40], dsm[:, 36:37], dsm[:, 35:36], ALU.add))
            step(V_.reciprocal(dsm[:, 40:41], dsm[:, 39:40]))
            V_.tensor_tensor(dsm[:, 41:42], dsm[:, 40:41], dcon[:, E_PAR:E_PAR + 1], ALU.mult)
            step(V_.tensor_tensor(dsm[:, 42:43], dsm[:, 40:41], dcon[:, E_PAR + 1:E_PAR + 2], ALU.mult))
            dve.wait_ge(pd_ps, 3)
            V_.tensor_copy(pself, ps[0:BD, 2, 256:384]).then_inc(dq_done, 1)
            u_phase(3, {1: [lambda: add_y(2)], 2: [lambda: copy_idxT(3)]})
            dve.wait_ge(k_used, 4 * NPG)
            step(V_.scalar_tensor_tensor(oX, ps[:, 4, :], dsm[:, 41:42], dcon[:, E_VE:E_VE + 512], ALU.mult, ALU.mult))
            step(V_.scalar_tensor_tensor(oY, ps[:, 5, :], dsm[:, 42:43], dcon[:, E_VE + 512:E_VE + 1024],
                                         ALU.mult, ALU.mult))
            V_.tensor_tensor(oX, oX, oY, ALU.add)
            step(V_.tensor_scalar(oL, ps[:, 6, 0:P], dsm[:, 41:42], None, ALU.mult))
            V_.scalar_tensor_tensor(oL, ps[:, 6, P:2 * P], dsm[:, 42:43], oL, ALU.mult, ALU.add).then_inc(oL_done, 1)
            dve.wait_ge(d_ps, 3)
            V_.tensor_copy(mxs[0:BD, 0:512], ps[0:BD, 3, :])
            V_.tensor_copy(mxs[0:BD, 512:1024], ps[0:BD, 2, :]).then_inc(dm_done, 1)
            rms_of(BD, ssa[0:BD, 1:3], 512)
            V_.tensor_scalar(mxs[0:BD, 0:512], mxs[0:BD, 0:512], rv[0:BD, 0:1], None, ALU.mult)
            V_.tensor_scalar(mxs[0:BD, 512:1024], mxs[0:BD, 512:1024], rv[0:BD, 1:2], None,
                             ALU.mult).then_inc(s_xn, 1)
            dve.wait_ge(s_tr, 1)
            V_.tensor_tensor(xTs, ps[:, 7, 0:64].rearrange("p (c t) -> p c t", c=DC),
                             gT[:, DC:2 * DC].unsqueeze(2).to_broadcast([P, DC, BD]), ALU.mult).then_inc(s_mT, 1)
            dve.wait_ge(s_op, 1)
            dve.wait_ge(sx_in, 16)
            for i in range(2):
                last = V_.tensor_tensor(hs[0:BD, i * 512:(i + 1) * 512], ps[0:BD, 2 + i, :],
                                        hs[0:BD, i * 512:(i + 1) * 512], ALU.add)
            last.then_inc(s_h, 1)
            rms_of(BD, ssa[0:BD, 3:4], D)
            V_.scalar_tensor_tensor(xs2, hs[0:BD, :], rv[0:BD, 0:1], gf[0:BD, :], ALU.mult, ALU.mult).then_inc(s_xn, 1)
            V_.tensor_copy(selT, ident[0:BD, 0:BD].unsqueeze(2).to_broadcast([BD, BD, P])).then_inc(selT_done, 1)
            dve.wait_ge(s_sc, 1)
            top_subkeys(SBLK, lambda hp: ps[0:BD, 2 + hp // 4, P * (hp % 4):P * (hp % 4) + P], 0, 16)
            top_experts(SBLK)
            copy_idxT(SBLK)
            V_.tensor_copy(dsm[:, 56:64], ps[:, 7, 8:16]).then_inc(s_gT, 1)
            add_y(3)
            for k in range(BD):
                q = 2 * P * NB + k
                dve.wait_ge(g[q % RING], 16 * (q // RING + 1))
                dve.wait_ge(s_xb, k + 1)
                V_.tensor_tensor_reduce(heads(ring[:, q % RING, :], P, 2), heads(ring[:, q % RING, :], P, 2),
                                        ps[:, 2 + 2 * (k % 2):4 + 2 * (k % 2), :], 1.0, 0.0, ALU.mult, ALU.add,
                                        acc[:, k:k + 1]).then_inc(s_u, 1)
            dve.wait_ge(gelu_done, NB + 1)
            w8 = W32[:, 0, 0:2, :].rearrange("p c m -> p (c m)")
            step(V_.memset(w8, 0.0))
            w8d = W32[:, 0, 0:2, :].rearrange("p c m -> p (c m)")[:, 0:64:9]
            V_.tensor_tensor(w8d, acc[:, 0:BD], dsm[:, 56:64], ALU.mult).then_inc(W_done, 1)
            dve.wait_ge(s_v, 1)
            for i in range(2):
                last = V_.tensor_tensor(hs[0:BD, i * 512:(i + 1) * 512], ps[0:BD, i, :],
                                        hs[0:BD, i * 512:(i + 1) * 512], ALU.add)
            last.then_inc(y_done, 1)

        @block.tensor
        def _(pe):
            T_ = nc.tensor
            pe.wait_ge(const_in, 16 * 3)

            def transposes(src, banks, n, done):
                for c in range(DC):
                    last = T_.transpose(ps[:, banks[c // 4], (c % 4) * n:(c % 4) * n + n],
                                        src[0:n, c * P:(c + 1) * P], ident[0:n, 0:n])
                last.then_inc(done, 1)

            def turn_x(t):
                pe.wait_ge(x_norm, t + 1)
                transposes(hb, (6, 7), ROWS[ORDER[t]], x_tr)

            def turn_mixture(b):
                pe.wait_ge(m_norm, b + 1)
                transposes(mx, (6, 7), P, m_tr)

            turn_x(0)
            for t, b in enumerate(ORDER):
                n = ROWS[b]
                pe.wait_ge(xnT_done, t + 1)

                def project_in(i, c):
                    w = 512 if i < 4 else TAIL
                    ins = T_.matmul(ps[0:n, i, 0:w], xnT[:, c, 0:n], win[:, c, 512 * i:512 * i + w],
                                    start=(c == 0), stop=(c == DC - 1))
                    if c == DC - 1:
                        ins.then_inc(proj_ps, 1)

                if t == 0:
                    for c in range(DC):
                        pe.wait_ge(win_in[c], 16)
                        for i in PROJ_ORDER:
                            project_in(i, c)
                    pe.wait_ge(const2_in, 16 * 4)
                    turn_x(1)
                    pe.wait_ge(xnT_done, 2)
                else:
                    if t == 1:
                        pe.wait_ge(qk_done, 1)
                        pe.wait_ge(v_done, 2)
                    for i in PROJ_ORDER:
                        if i == 0 and t > 1:
                            turn_mixture(b - 1)
                            pe.wait_ge(mx_done, b)
                        for c in range(DC):
                            project_in(i, c)
                pe.wait_ge(ckv_done, t + 1)
                T_.transpose(ps[:, 7, 0:n], ckvn[0:n, :], ident[0:n, 0:n]).then_inc(ckv_ps, 1)
                pe.wait_ge(ckvT_done, t + 1)
                T_.matmul(ps[0:n, 5, :], ckvT[:, 0:n], wk, start=True, stop=True)
                T_.matmul(ps[0:n, 6, :], ckvT[:, 0:n], wv, start=True, stop=True).then_inc(kv_ps, 1)
                if b == SBLK:
                    continue
                pe.wait_ge(lf_done, t + 1)
                for a in range(b + 1):
                    lhs = con[:, C_TRI:C_TRI + P] if a == b else con[:, C_ONES:C_ONES + P]
                    last = T_.matmul(ps[:, 7, 256:256 + H], lhs, lf[:, a, :], start=(a == 0), stop=(a == b))
                last.then_inc(c_ps, 1)
                pe.wait_ge(qk_done, t + 1)
                pe.wait_ge(v_done, 2 * (t + 1))
                for gi in range(8):
                    kd, fox = (KM, 0) if gi % 4 < 2 else (KF, 1)
                    src = Qk if gi < 4 else Kk
                    for j in range(4):
                        h = 4 * (gi % 2) + j
                        o = (H * KM if fox else 0) + h * kd
                        last = T_.transpose(ps[0:kd, QKB[gi], j * P:(j + 1) * P], src[:, o:o + kd], ident)
                    last.then_inc(qk_ps, 1)
                pe.wait_ge(qk_even, 4 * (b + 1))
                pe.wait_ge(qk_odd, 4 * (b + 1))
                w = (b + 1) * P

                def scores(hh):
                    kd = KM if hh < 8 else KF
                    if hh >= 2:
                        pe.wait_ge(exp_done, 16 * b + hh - 1)
                    T_.matmul(ps[:, 2 + hh % 2, 0:w], QT[0:kd, hh, :], KT[0:kd, hh, 0:w],
                              start=True, stop=True).then_inc(s_ps, 1)

                def turn(hh):
                    pe.wait_ge(exp_done, 16 * b + hh + 1)
                    if hh >= 2:
                        pe.wait_ge(pT_done[hh % 2], 8 * b + hh // 2)
                    for a in range(b + 1):
                        last = T_.transpose(ps[:, 4 + hh % 2, a * P:(a + 1) * P], Pm[:, hh % 2, a * P:(a + 1) * P],
                                            ident)
                    last.then_inc(pT_ps, 1)

                def values(hh):
                    pe.wait_ge(pT_done[hh % 2], 8 * b + hh // 2 + 1)
                    for a in range(b + 1):
                        last = T_.matmul(ps[:, hh // 8, VD * (hh % 8):VD * (hh % 8) + VD],
                                         PT[:, hh % 2, a * P:(a + 1) * P], V[:, a, VD * hh:VD * hh + VD],
                                         start=(a == 0), stop=(a == b))
                    last.then_inc(o_ps, 1)

                scores(0)
                for hh in range(16):
                    if hh + 1 < 16:
                        scores(hh + 1)
                    turn(hh)
                    if hh:
                        values(hh - 1)
                    if t < NB and hh == 10:
                        turn_x(t + 1)
                values(15)
            turn_mixture(NB - 1)

            pe.wait_ge(wo_in, 16 * DC)

            def project(b):
                if b:
                    pe.wait_ge(sc_done, 4 * b)
                pe.wait_ge(mixT_done, b + 1)
                for i in range(2):
                    for c in range(DC):
                        last = T_.matmul(ps[:, i, :], mixT[:, b, c, :], wo[:, c, 512 * i:512 * i + 512],
                                         start=(c == 0), stop=(c == DC - 1))
                last.then_inc(op_ps, 1)

            def route(b):
                pe.wait_ge(xn2_done, b + 1)
                transposes(xn2[:, b, :], (6, 7), P, tr_ps)
                pe.wait_ge(xnT2_done, b + 1)
                if b == 0:
                    pe.wait_ge(wq_in, 16 * DC)
                    pe.wait_ge(sk_in, 16)

                def queries(i):
                    for hp in range(4 * i, 4 * i + 4):
                        for c in range(DC):
                            last = T_.matmul(ps[:, 2 + i, P * (hp % 4):P * (hp % 4) + P],
                                             wq[:, c, P * hp:P * hp + P], hb[:, c * P:(c + 1) * P],
                                             start=(c == 0), stop=(c == DC - 1))
                    last.then_inc(q_ps, 1)

                def subkey_scores(i):
                    pe.wait_ge(q_done, 4 * b + i + 1)
                    for hp in range(4 * i, 4 * i + 4):
                        last = T_.matmul(ps[:, SCB[i], P * (hp % 4):P * (hp % 4) + P], qpT[:, hp, :],
                                         skT[:, hp, :], start=True, stop=True)
                    last.then_inc(sc_ps, 1)

                queries(0)
                for i in range(1, 4):
                    queries(i)
                    subkey_scores(i - 1)
                subkey_scores(3)

            for b in range(NB):
                project(b)
                route(b)

            def turn_idx(b):
                n = ROWS[b]
                pe.wait_ge(top_done, b + 1)
                pe.wait_ge(sc_done, 4 * NB)
                if b:
                    pe.wait_ge(W_done, b)
                T_.transpose(ps[:, 7, 0:n], eidf[0:n, :], ident[0:n, 0:n]).then_inc(idx_ps, 1)

            def turn_w(b):
                pe.wait_ge(w_done, b + 1)
                pe.wait_ge(idxT_done, b + 1)
                T_.transpose(ps[:, 7, 0:P], acc[:, :], ident).then_inc(w_ps, 1)

            def v_phase(b, between={}):
                pe.wait_ge(W_done, b + 1)
                if b:
                    pe.wait_ge(y_done, b)
                for k in range(P):
                    q = 2 * P * b + P + k
                    c, j = k // 4, k % 4
                    if k in between:
                        between[k]()
                    pe.wait_ge(g[q % RING], 16 * (q // RING + 1))
                    for i in range(2):
                        last = T_.matmul(ps[32 * j:32 * j + 32, i, :], W32[:, j, c, :],
                                         ring[:, q % RING, 512 * i:512 * i + 512], start=(c == 0), stop=(c == 31),
                                         tile_position=(0, 32 * j), skip_group_check=True)
                    last.then_inc(v_used, 1)

            turn_idx(0)
            def turn_decode_queries():
                pe.wait_ge(dq_in, 1)
                for c in range(8):
                    T_.transpose(ps[:, 6, 8 * c:8 * c + 8], SR[0:BD, 2048 + P * c:2048 + P * (c + 1)], ident[0:BD, 0:BD])
                for h in range(H):
                    last = T_.transpose(ps[0:RP, 6, 64 + 8 * h:72 + 8 * h], SB[0:BD, KM * h + NOPE:KM * (h + 1)],
                                        ident[0:BD, 0:BD])
                last.then_inc(d_ps, 1)

            def absorb_decode_queries():
                pe.wait_ge(dq_in, 2)
                for i in range(2):
                    T_.matmul(ps[:, 6, 128 + i:129 + i], dsm[0:BD, 64 + 128 * i:192 + 128 * i],
                              con[0:BD, C_ONES:C_ONES + 1], start=True, stop=True)
                for q in range(4):
                    last = T_.matmul(ps[:, 6, 256 + 16 * q:272 + 16 * q], wkTd[:, q, :], qbd[:, q, :],
                                     start=True, stop=True)
                last.then_inc(d_ps, 1)

            def decode_scores(first, last_it):
                with pe.Fori(first, last_it) as it:
                    for s in range(2):

                        def key_norm(par, q):
                            m = (2 * s + par) * 4 + q
                            pe.wait_ge(sqd_done, pe.snap(it * 16 + (m + 1)))
                            T_.matmul(ps[:, 2 + q % 2, :], wkd[:, q * P:(q + 1) * P], kbuf[:, par, :, 512:640],
                                      start=True, stop=True).then_inc(n_ps, 1)

                        def norm_sum(par, q, final=None):
                            m = (2 * s + par) * 4 + q
                            pe.wait_ge(sqd_done, pe.snap(it * 16 + (m + 3)))
                            for j in range(4):
                                last = T_.matmul(ps[32 * j:32 * j + 32, 4 + s, 2 * P:3 * P],
                                                 dcon[:, E_HM + 32 * (4 * par + q):E_HM + 32 * (4 * par + q) + 32],
                                                 sqd[:, q % 2, j * P:(j + 1) * P],
                                                 start=False, stop=(par == 1 and q == 3),
                                                 tile_position=(0, 32 * j), skip_group_check=True)
                            last.then_inc(sqd_used, 1)

                        pe.wait_ge(abr_done, pe.snap(it * 2 + (s + 1)))
                        pe.sem_inc(tensor_waited, 1)
                        for par in range(2):
                            pe.wait_ge(k_in[par], pe.snap(it * 256 + (128 * s + 128)))
                            pe.sem_inc(tensor_waited, 1)
                            key_norm(par, 0)
                            key_norm(par, 1)
                            for c in range(4):
                                for j in range(4):
                                    T_.matmul(ps[32 * j:32 * j + 32, 4 + s, 0:P], qz[:, c, 2 * j + par, :],
                                              kbuf[:, par, j, c * P:(c + 1) * P], start=(par == 0 and c == 0),
                                              stop=False, tile_position=(0, 32 * j), skip_group_check=True)
                            norm_sum(par, 0)
                            key_norm(par, 2)
                            for j in range(4):
                                T_.matmul(ps[32 * j:32 * j + 32, 4 + s, P:2 * P], qz[:, 4, 2 * j + par, :],
                                          kbuf[:, par, j, 512:640], start=False, stop=(par == 1),
                                          tile_position=(0, 32 * j), skip_group_check=True)
                            norm_sum(par, 1)
                            key_norm(par, 3)
                            for j in range(4):
                                last = T_.matmul(ps[32 * j:32 * j + 32, 4 + s, 0:P], qpz[0:RP, 2 * j + par, :],
                                                 kpb[0:RP, par, j, :], start=False, stop=(par == 1),
                                                 tile_position=(0, 32 * j), skip_group_check=True)
                            last.then_inc(k_used, 1)
                            norm_sum(par, 2)
                            norm_sum(par, 3)

            def first_scores():
                pe.wait_ge(dq_done, 2)
                decode_scores(0, 1)

            pe.sem_inc(sqd_used, 2)
            turn_w(0)
            v_phase(0, {16: turn_decode_queries, 24: absorb_decode_queries, 40: first_scores})
            turn_idx(1)
            decode_scores(1, 8)
            turn_w(1)
            v_phase(1, {40: lambda: decode_scores(8, 9)})
            turn_idx(2)
            decode_scores(9, 16)
            turn_w(2)
            v_phase(2)
            turn_idx(3)
            pe.sem_inc(pd_ps, 2)
            pe.wait_ge(dq_done, 3)
            T_.transpose(ps[0:BD, 2, 256:384], dsm[:, 48:56], ident).then_inc(pd_ps, 1)
            pe.wait_ge(dq_done, 4)
            pe.wait_ge(v_in, 48)
            for k in range(2):
                T_.matmul(ps[:, 4 + k, :], pself, sqd[0:BD, 0, :], start=True, stop=False, skip_group_check=True)
            T_.matmul(ps[:, 6, 0:2 * P], pself, sqd[0:BD, 1, 0:R].unsqueeze(1).to_broadcast([BD, 2, R]),
                      start=True, stop=False, skip_group_check=True)
            with pe.Fori(0, NPG // 2) as it:
                for s in range(2):
                    pe.wait_ge(stg_done, pe.snap(it * 2 + (s + 1)))
                    pe.sem_inc(tensor_waited, 1)
                    pe.wait_ge(pd_done, pe.snap(it * 2 + (s + 1)))
                    T_.transpose(ps[:, 2 + s, 0:P], stg[:, s, :], ident).then_inc(pd_ps, 1)
                    pe.wait_ge(pd_done, pe.snap(it * 2 + (s + 3)))
                    pe.sem_inc(tensor_waited, 1)
                    for par in range(2):
                        pe.wait_ge(k_in[par], pe.snap(it * 128 + (128 * NPG + 64 * s + 64)))
                        pe.sem_inc(tensor_waited, 1)
                        for j in range(4):
                            T_.matmul(ps[32 * j:32 * j + 32, 4 + par, :], pTd[:, s, 32 * j:32 * j + 32],
                                      kbuf[:, par, j, 0:512], start=False, stop=True,
                                      tile_position=(0, 32 * j), skip_group_check=True)
                        for j in range(4):
                            last = T_.matmul(ps[32 * j:32 * j + 32, 6, par * P:(par + 1) * P],
                                             pTd[:, s, 32 * j:32 * j + 32], kbuf[:, par, j, 512:640],
                                             start=False, stop=True, tile_position=(0, 32 * j),
                                             skip_group_check=True)
                        last.then_inc(k_used, 1)
            turn_w(3)

            def turn_latents():
                pe.wait_ge(oL_done, 1)
                T_.transpose(ps[:, 7, 0:P], oL, ident).then_inc(oLT_ps, 1)

            def heads_by_token():
                pe.wait_ge(s_sum, 1)
                T_.matmul(ps[0:BD, 2, :], dcon[:, E_B:E_B + BD], oX, start=True, stop=True)
                for h in range(H):
                    last = T_.matmul(ps[0:BD, 3, VD * h:VD * h + VD], oLT[:, 8 + h::16], wvs[:, VD * h:VD * h + VD],
                                     start=True, stop=True)
                last.then_inc(d_ps, 1)

            def turn_s(rows, count):
                pe.wait_ge(s_xn, count)
                for c in range(DC):
                    last = T_.transpose(ps[:, 7, 8 * c:8 * c + 8], rows[:, c * P:(c + 1) * P], ident[0:BD, 0:BD])
                last.then_inc(s_tr, 1)

            def project_s(i):
                if i == 0:
                    pe.wait_ge(s_mT, 1)
                    pe.wait_ge(swo_in, 16 * DC)
                for c in range(DC):
                    last = T_.matmul(ps[0:BD, 2 + i, :], xTs[:, c, :], wo_s[:, c, 512 * i:512 * i + 512],
                                     start=(c == 0), stop=(c == DC - 1))
                if i == 1:
                    last.then_inc(s_op, 1)

            def queries_s(lo, hi):
                if lo == 0:
                    pe.wait_ge(s_xT, 1)
                    pe.wait_ge(swq_in, 16 * DC)
                for c in range(lo, hi):
                    for j in range(4):
                        last = T_.matmul(ps[32 * j:32 * j + BD, 6, :], xTs[:, c, :], wq_s[c][:, 512 * j:512 * j + 512],
                                         start=(c == 0), stop=(c == DC - 1), tile_position=(0, 32 * j),
                                         skip_group_check=True)
                if hi == DC:
                    last.then_inc(s_q, 1)

            def turn_queries_s():
                pe.wait_ge(s_qr, 1)
                for m in range(4):
                    last = T_.transpose(ps[:, 7, m * P:(m + 1) * P], qrow[:, m * P:(m + 1) * P], ident)
                last.then_inc(s_qt, 1)

            def scores_s():
                pe.wait_ge(s_qT, 1)
                pe.wait_ge(ssk_in, 16)
                for hp in range(NHP):
                    last = T_.matmul(ps[0:BD, 2 + hp // 4, P * (hp % 4):P * (hp % 4) + P], qTs[:, hp, :],
                                     skT_s[:, hp, :], start=True, stop=True)
                last.then_inc(s_sc, 1)

            def turn_experts_s():
                pe.wait_ge(gates_done, NB + 1)
                T_.transpose(ps[:, 7, 8:16], gate[0:BD, 0, :], ident[0:BD, 0:BD])
                turn_idx(SBLK)

            def spread_s(k):
                if k == 0:
                    pe.wait_ge(selT_done, 1)
                    pe.wait_ge(s_gT, 1)
                if k >= 2:
                    pe.wait_ge(s_u, k - 1)
                for i in range(2):
                    last = T_.matmul(ps[:, 2 + 2 * (k % 2) + i, :], selT[:, k, :], xs2[:, 512 * i:512 * i + 512],
                                     start=True, stop=True)
                last.then_inc(s_xb, 1)

            v_phase(3, {4: turn_latents, 8: heads_by_token, 16: lambda: turn_s(mxs[0:BD, :], 1), 22: lambda: project_s(0), 26: lambda: project_s(1),
                        32: lambda: turn_s(xs2, 2), 40: lambda: queries_s(0, 4), 42: lambda: queries_s(4, 8),
                        48: turn_queries_s, 54: scores_s, 116: turn_experts_s})
            for k in range(BD):
                spread_s(k)
            pe.wait_ge(W_done, NB + 1)
            pe.wait_ge(y_done, NB)
            w8 = W32[:, 0, 0:2, :].rearrange("p c m -> p (c m)")
            for k in range(BD):
                q = 2 * P * NB + BD + k
                pe.wait_ge(g[q % RING], 16 * (q // RING + 1))
                for i in range(2):
                    last = T_.matmul(ps[0:BD, i, :], w8[:, 8 * k:8 * k + 8],
                                     ring[:, q % RING, 512 * i:512 * i + 512], start=(k == 0), stop=(k == BD - 1))
            last.then_inc(s_v, 1)


_OUTS = [
    ((1, T, D)), ((BD, 1, D)), ((1, 1, T, R)), ((1, 1, T, RP)), ((1, 1, T, H, FD)), ((1, 1, T, H, FD)), ((1, 1, T, H)),
    ((1, BD, 1, R)), ((1, BD, 1, RP)), ((1, BD, 1, H, FD)), ((1, BD, 1, H, FD)), ((1, BD, 1, H)),
]
_FLAT = [(T, D), (BD, D), (T, R), (T, RP), (T, H * FD), (T, H * FD), (T, H),
         (BD, R), (BD, RP), (BD, H * FD), (BD, H * FD), (BD, H)]
_NAMES = ["y_prompt", "y_sample", "lat_p", "kpe_p", "fk_p", "fv_p", "lf_p", "lat_s", "kpe_s", "fk_s", "fv_s", "lf_s"]


def _constants():
    c = np.zeros((P, C_END), np.float32)
    i, j = np.arange(P)[:, None], np.arange(P)[None, :]
    c[:, C_ID:C_ID + P] = i == j
    c[:, C_MASK:C_MASK + P] = np.where(j <= i, 0.0, NEG)
    c[:, C_TRI:C_TRI + P] = i <= j
    c[:, C_ONES:C_ONES + P] = 1.0
    half = RP // 2
    inv = np.power(np.float32(10000.0), -np.arange(half, dtype=np.float32) / np.float32(half)).astype(np.float32)
    pos = np.stack([np.arange(P) + b * P for b in range(NB)] + [np.full(P, PAST)], 1).astype(np.float32)
    ang = pos[:, :, None] * inv
    c[:, C_COS:C_SIN] = np.cos(ang).reshape(P, -1)
    c[:, C_SIN:C_DIM] = np.sin(ang).reshape(P, -1)
    c[:, C_DIM:C_IOTA] = [1.0 / NOPE] * 24 + [1.0 / RP] * 8 + [1.0 / R, 1.0 / RP]
    c[:, C_IOTA:C_END] = np.arange(16)
    return c


def _decode_constants():
    e = np.zeros((P, E_END), np.float32)
    for par in range(2):
        for q in range(4):
            for half in range(2):
                e[64 * half:64 * half + 64, E_HM + 32 * (4 * par + q) + 16 * par + 8 + 2 * q + half] = 1.0
    for row in range(P):
        b, h = row // 16, row % 16
        e[b, E_BT + row] = 1.0
        e[row, E_B + b] = 1.0
        if h < H:
            a = E_VE + 512 * (b % 2) + FD * h
            e[row, a:a + FD] = 1.0
        e[row, E_PAR + b % 2] = 1.0
        e[row, E_MOD] = h
    return e


def _layout(x_prompt, x_sample, cache_mla_latent, cache_mla_kpe, cache_fox_k, cache_fox_v, cache_fox_logf,
            page_table, g_attn, w_in, b_forget, g_q_nope, g_q_pe, g_ckv, g_k_pe, w_ukv, g_k_nope,
            g_fox_q, g_fox_k, g_out_mla, g_out_fox, w_o, g_ffn, w_peer_q, peer_sub_keys, peer_u, peer_v):
    n = cache_mla_latent.shape[1]
    cols = np.split(w_in[0], np.cumsum([512, 256, 128, 32, 512, 512, 512]), axis=1)
    win = np.concatenate([cols[0], cols[4], cols[5], cols[6], cols[1], cols[2], cols[3], cols[7]], axis=1)
    ukv = w_ukv[0].reshape(R, H, NOPE + VD)
    w_k = np.ascontiguousarray(ukv[:, :, :NOPE]).reshape(R, H * NOPE)
    w_v = np.ascontiguousarray(ukv[:, :, NOPE:]).reshape(R, H * VD)
    chunks = lambda w: w.reshape(DC, P, -1).transpose(1, 0, 2)
    lat, fox_k = cache_mla_latent[0], cache_fox_k[0].reshape(n, PAGE, 4, P)
    fox_v = cache_fox_v[0].reshape(n, PAGE, H * FD)
    logf = np.zeros((n, 16, PAGE), np.float32)
    logf[:, :H] = cache_fox_logf[0].transpose(0, 2, 1)
    pages = page_table.reshape(4, 2, NPG).transpose(2, 1, 0).reshape(1, -1)
    return {
        "x_prompt": x_prompt.reshape(T, D), "x_sample": x_sample.reshape(BD, D),
        "w_in": chunks(win), "w_k": w_k, "w_v": w_v,
        "w_kT": w_k.T.reshape(4, P, R).transpose(1, 0, 2),
        "w_o": chunks(w_o[0]), "w_q": chunks(w_peer_q[0]),
        "sub_keys": peer_sub_keys[0].reshape(NHP, P, P).transpose(2, 0, 1),
        "gains": np.concatenate([g_q_nope[0], g_q_pe[0], g_ckv[0], g_k_pe[0], g_k_nope[0], g_fox_q[0], g_fox_k[0],
                                 b_forget[0]]),
        "g_cols": np.concatenate([g_attn[0].reshape(DC, P), g_out_mla[0].reshape(4, P), g_out_fox[0].reshape(4, P)]).T,
        "g_ffn": g_ffn[0], "consts": _constants(), "dec_consts": _decode_constants(),
        "pages": pages, "page_rows": np.repeat(page_table, 16, axis=0),
        "kt_pool": np.concatenate([fox_k.transpose(0, 3, 2, 1).reshape(n, P, 4 * PAGE), lat.transpose(0, 2, 1)], axis=2),
        "kpe_pool": cache_mla_kpe[0].transpose(0, 2, 1),
        "vn_pool": np.concatenate([fox_v, lat], axis=2),
        "logf_pool": logf.reshape(n * 16, PAGE),
        "peer_u": peer_u[0], "peer_v": peer_v[0],
    }


def kernel(**inputs):
    import concourse.bacc as bacc
    from concourse.bass_utils import run_bass_kernel_spmd

    arrays = {k: np.ascontiguousarray(v) for k, v in _layout(**{k: np.asarray(v) for k, v in inputs.items()}).items()}
    nc = bacc.Bacc("TRN2", target_bir_lowering=False, num_devices=1)
    args = {k: nc.dram_tensor(k, a.shape, mybir.dt.from_np(a.dtype), kind="ExternalInput").ap()
            for k, a in arrays.items()}
    for name, shape in zip(_NAMES, _FLAT):
        args[name] = nc.dram_tensor(name, shape, F32, kind="ExternalOutput").ap()
    build(nc, **args)
    got = run_bass_kernel_spmd(nc, [arrays], core_ids=[0]).results[0]
    return tuple(got[name].reshape(shape) for name, shape in zip(_NAMES, _OUTS))
```
